# Optimizing a Trainium2 kernel written in Bass

```python
import math
import jax
import jax.numpy as jnp
from jax import lax
import numpy as np

D_MODEL = 1024
BATCH = 1
SEQ = 512
DEPTH = 2

N_MIXERS = 2
N_RET_LAYERS = (DEPTH + 1) // 2
N_CONV_LAYERS = DEPTH // 2
RET_HEADS = 4
RET_DK = 256
RET_DV = 512
RET_QK = RET_HEADS * RET_DK
RET_V = RET_HEADS * RET_DV
RET_IN = 2 * RET_QK + 2 * RET_V
RET_CHUNK = 128
ROPE_BASE = 10000.0
CONV_WIDTH = 31
MOE_GROUPS = 4
MOE_EXPERTS_PER_GROUP = 8
MOE_EXPERTS = MOE_GROUPS * MOE_EXPERTS_PER_GROUP
MOE_TOPK = 2
MOE_FF = 512
MOE_BLOCK = 128
NORM_EPS = 1e-6

kernel_name = "hybrid_retention_conformer_hmoe"

def rmsnorm(x, g):
    xf = x.astype(jnp.float32)
    y = xf * lax.rsqrt(jnp.mean(xf * xf, axis=-1, keepdims=True) + NORM_EPS)
    return (y * g.astype(jnp.float32)).astype(x.dtype)

def rotary(t, positions):
    half = t.shape[-1] // 2
    inv = ROPE_BASE ** (-jnp.arange(half, dtype=jnp.float32) / half)
    ang = positions.astype(jnp.float32)[:, :, None] * inv
    cos = jnp.cos(ang)[:, :, None, :]
    sin = jnp.sin(ang)[:, :, None, :]
    t1 = t[..., :half].astype(jnp.float32)
    t2 = t[..., half:].astype(jnp.float32)
    return jnp.concatenate([t1 * cos - t2 * sin, t1 * sin + t2 * cos], axis=-1).astype(t.dtype)

def retention_mixer(h, positions, w_in, head_g, w_out):
    B, S, _ = h.shape
    dt = h.dtype
    proj = h @ w_in
    q, k, v, g = jnp.split(proj, [RET_QK, 2 * RET_QK, 2 * RET_QK + RET_V], axis=-1)
    q = rotary(q.reshape(B, S, RET_HEADS, RET_DK), positions)
    k = rotary(k.reshape(B, S, RET_HEADS, RET_DK), positions) * (RET_DK ** -0.5)
    v = v.reshape(B, S, RET_HEADS, RET_DV)

    n_chunks = S // RET_CHUNK

    def to_chunks(t):
        return t.reshape(B, n_chunks, RET_CHUNK, RET_HEADS, t.shape[-1]).transpose(1, 0, 3, 2, 4)

    log_gamma = jnp.log1p(-(2.0 ** (-5.0 - jnp.arange(RET_HEADS, dtype=jnp.float32))))
    idx = jnp.arange(RET_CHUNK, dtype=jnp.float32)
    diff = idx[:, None] - idx[None, :]
    intra = jnp.where(diff >= 0, jnp.exp(log_gamma[:, None, None] * jnp.maximum(diff, 0.0)), 0.0).astype(dt)
    cross_dec = jnp.exp(log_gamma[:, None] * (idx + 1.0)).astype(dt)
    k_dec = jnp.exp(log_gamma[:, None] * (RET_CHUNK - 1.0 - idx)).astype(dt)
    chunk_dec = jnp.exp(log_gamma * RET_CHUNK).astype(dt)

    def step(state, qkv):
        qc, kc, vc = qkv
        scores = jnp.einsum('bhid,bhjd->bhij', qc, kc) * intra[None]
        o_inner = jnp.einsum('bhij,bhjv->bhiv', scores, vc)
        o_cross = jnp.einsum('bhid,bhdv->bhiv', qc, state) * cross_dec[None, :, :, None]
        new_state = state * chunk_dec[None, :, None, None] + jnp.einsum(
            'bhjd,bhjv->bhdv', kc * k_dec[None, :, :, None], vc)
        return new_state, o_inner + o_cross

    state0 = jnp.zeros((B, RET_HEADS, RET_DK, RET_DV), dt)
    _, o = lax.scan(step, state0, (to_chunks(q), to_chunks(k), to_chunks(v)))
    o = o.transpose(1, 0, 3, 2, 4).reshape(B, S, RET_HEADS, RET_DV)
    of = o.astype(jnp.float32)
    of = of * lax.rsqrt(jnp.mean(of * of, axis=-1, keepdims=True) + NORM_EPS)
    of = of * head_g.astype(jnp.float32).reshape(RET_HEADS, RET_DV)
    o = of.reshape(B, S, RET_V).astype(dt)
    return (jax.nn.silu(g) * o) @ w_out

def conformer_conv_mixer(h, w_pw1, b_pw1, w_dw, b_dw, ln_g, ln_b, w_pw2, b_pw2):
    D = h.shape[-1]
    u = h @ w_pw1 + b_pw1
    a, gate = jnp.split(u, 2, axis=-1)
    u = a * jax.nn.sigmoid(gate)
    z = lax.conv_general_dilated(
        u, w_dw[:, None, :].astype(u.dtype), window_strides=(1,),
        padding=[(CONV_WIDTH - 1, 0)], dimension_numbers=('NWC', 'WIO', 'NWC'),
        feature_group_count=D) + b_dw
    zf = z.astype(jnp.float32)
    mu = jnp.mean(zf, axis=-1, keepdims=True)
    var = jnp.mean(jnp.square(zf - mu), axis=-1, keepdims=True)
    zf = (zf - mu) * lax.rsqrt(var + NORM_EPS) * ln_g.astype(jnp.float32) + ln_b.astype(jnp.float32)
    z = jax.nn.silu(zf).astype(h.dtype)
    return z @ w_pw2 + b_pw2

def hierarchical_moe(h, w_rg, b_rg, w_re, b_re, w_gate, w_up, w_down):
    B, S, D = h.shape
    N = B * S
    xt = h.reshape(N, D)
    lg = (xt @ w_rg + b_rg).astype(jnp.float32)
    pg = jax.nn.softmax(lg, axis=-1)
    g_idx = jnp.argmax(lg, axis=-1).astype(jnp.int32)
    gate_g = jnp.take_along_axis(pg, g_idx[:, None], axis=-1)
    le = (xt @ w_re + b_re).astype(jnp.float32).reshape(N, MOE_GROUPS, MOE_EXPERTS_PER_GROUP)
    le_sel = jnp.take_along_axis(le, g_idx[:, None, None], axis=1)[:, 0]
    top_v, top_i = lax.top_k(le_sel, MOE_TOPK)
    pe = jax.nn.softmax(top_v, axis=-1)
    wts = (gate_g * pe).reshape(-1)
    eid = (g_idx[:, None] * MOE_EXPERTS_PER_GROUP + top_i.astype(jnp.int32)).reshape(-1)
    A = N * MOE_TOPK
    tok = jnp.arange(A, dtype=jnp.int32) // MOE_TOPK
    order = jnp.argsort(eid, stable=True)
    e_s, tok_s, w_s = eid[order], tok[order], wts[order]
    counts = jnp.bincount(eid, length=MOE_EXPERTS).astype(jnp.int32)
    pcounts = (counts + MOE_BLOCK - 1) // MOE_BLOCK * MOE_BLOCK
    start = jnp.cumsum(counts) - counts
    pend = jnp.cumsum(pcounts)
    pstart = pend - pcounts
    dest = pstart[e_s] + (jnp.arange(A, dtype=jnp.int32) - start[e_s])
    P = -(-A // MOE_BLOCK) * MOE_BLOCK + MOE_EXPERTS * MOE_BLOCK
    n_blocks = P // MOE_BLOCK
    buf_tok = jnp.full((P,), N, jnp.int32).at[dest].set(tok_s)
    buf_w = jnp.zeros((P,), jnp.float32).at[dest].set(w_s)
    blk_e = jnp.clip(jnp.searchsorted(pend, jnp.arange(n_blocks, dtype=jnp.int32) * MOE_BLOCK,
                                      side='right'), 0, MOE_EXPERTS - 1).astype(jnp.int32)
    x_pad = jnp.concatenate([xt, jnp.zeros((1, D), xt.dtype)], axis=0)
    xb = x_pad[buf_tok].reshape(n_blocks, MOE_BLOCK, D)

    def run_block(args):
        xblk, e = args
        return (jax.nn.silu(xblk @ w_gate[e]) * (xblk @ w_up[e])) @ w_down[e]

    yb = lax.map(run_block, (xb, blk_e)).reshape(P, D)
    out = jax.ops.segment_sum(yb * buf_w[:, None].astype(yb.dtype), buf_tok, num_segments=N + 1)[:N]
    return out.reshape(B, S, D).astype(h.dtype)

def setup_inputs(seed: int = 0) -> dict:
    key = jax.random.key(seed)
    ks = iter(jax.random.split(key, 32))
    D = D_MODEL
    f32 = jnp.float32

    def nrm(shape, scale):
        return jax.random.normal(next(ks), shape, f32) * scale

    x = jax.random.normal(next(ks), (BATCH, SEQ, D), f32)
    offs = jax.random.randint(next(ks), (BATCH, 1), 0, 1024, dtype=jnp.int32)
    positions = (jnp.arange(SEQ, dtype=jnp.int32)[None, :] + offs).astype(jnp.int32)
    return {
        "x": x,
        "positions": positions,
        "norm_mix_g": 1.0 + nrm((DEPTH, D), 0.01),
        "norm_ffn_g": 1.0 + nrm((DEPTH, D), 0.01),
        "ret_w_in": nrm((N_RET_LAYERS, D, RET_IN), D ** -0.5),
        "ret_head_g": 1.0 + nrm((N_RET_LAYERS, RET_V), 0.01),
        "ret_w_out": nrm((N_RET_LAYERS, RET_V, D), RET_V ** -0.5),
        "conv_w_pw1": nrm((N_CONV_LAYERS, D, 2 * D), D ** -0.5),
        "conv_b_pw1": nrm((N_CONV_LAYERS, 2 * D), 0.01),
        "conv_w_dw": nrm((N_CONV_LAYERS, CONV_WIDTH, D), CONV_WIDTH ** -0.5),
        "conv_b_dw": nrm((N_CONV_LAYERS, D), 0.01),
        "conv_ln_g": 1.0 + nrm((N_CONV_LAYERS, D), 0.01),
        "conv_ln_b": nrm((N_CONV_LAYERS, D), 0.01),
        "conv_w_pw2": nrm((N_CONV_LAYERS, D, D), D ** -0.5),
        "conv_b_pw2": nrm((N_CONV_LAYERS, D), 0.01),
        "moe_w_rg": nrm((DEPTH, D, MOE_GROUPS), D ** -0.5),
        "moe_b_rg": nrm((DEPTH, MOE_GROUPS), 0.01),
        "moe_w_re": nrm((DEPTH, D, MOE_EXPERTS), D ** -0.5),
        "moe_b_re": nrm((DEPTH, MOE_EXPERTS), 0.01),
        "moe_w_gate": nrm((DEPTH, MOE_EXPERTS, D, MOE_FF), D ** -0.5),
        "moe_w_up": nrm((DEPTH, MOE_EXPERTS, D, MOE_FF), D ** -0.5),
        "moe_w_down": nrm((DEPTH, MOE_EXPERTS, MOE_FF, D), MOE_FF ** -0.5),
        "final_norm_g": 1.0 + nrm((D,), 0.01),
    }

def reference(x, positions, norm_mix_g, norm_ffn_g, ret_w_in, ret_head_g, ret_w_out,
              conv_w_pw1, conv_b_pw1, conv_w_dw, conv_b_dw, conv_ln_g, conv_ln_b,
              conv_w_pw2, conv_b_pw2, moe_w_rg, moe_b_rg, moe_w_re, moe_b_re,
              moe_w_gate, moe_w_up, moe_w_down, final_norm_g):
    for i in range(DEPTH):
        h = rmsnorm(x, norm_mix_g[i])
        if i % N_MIXERS == 0:
            j = i // N_MIXERS
            x = x + retention_mixer(h, positions, ret_w_in[j], ret_head_g[j], ret_w_out[j])
        else:
            j = i // N_MIXERS
            x = x + conformer_conv_mixer(h, conv_w_pw1[j], conv_b_pw1[j], conv_w_dw[j], conv_b_dw[j],
                                         conv_ln_g[j], conv_ln_b[j], conv_w_pw2[j], conv_b_pw2[j])
        h = rmsnorm(x, norm_ffn_g[i])
        x = x + hierarchical_moe(h, moe_w_rg[i], moe_b_rg[i], moe_w_re[i], moe_b_re[i],
                                 moe_w_gate[i], moe_w_up[i], moe_w_down[i])
    return rmsnorm(x, final_norm_g)


_drawn_inputs = setup_inputs


def setup_inputs(seed=0):
    import zlib

    import numpy as np

    out = dict(_drawn_inputs(seed))
    spreads = {}
    factors = {'ret_head_g': 12.794,
     'conv_b_pw1': 3.908,
     'conv_b_dw': 3.539,
     'conv_ln_g': 33.315,
     'conv_ln_b': 32.31,
     'conv_b_pw2': 21.432,
     'moe_b_rg': 15.118,
     'final_norm_g': 32.057,
     'norm_ffn_g': 5.572,
     'moe_b_re': 4.593}
    for name, (base, spread) in spreads.items():
        noise = np.random.default_rng([zlib.crc32(name.encode()), seed]).standard_normal(out[name].shape)
        drawn = base * np.exp(spread * noise) if base else spread * noise
        out[name] = jnp.asarray(drawn.astype(out[name].dtype))
    for name, factor in factors.items():
        out[name] = (out[name] * factor).astype(out[name].dtype)
    return out
```

```python
from contextlib import ExitStack

import numpy as np
import concourse.bass as bass
from concourse import mybir

ALU = mybir.AluOpType
ACT = mybir.ActivationFunctionType
F32 = mybir.dt.float32
I32 = mybir.dt.int32
U32 = mybir.dt.uint32
AX = mybir.AxisListType.X

P = 128
S = 512
D = 1024
NT = S // P
KT = D // P
HEADS, DK, DV = 4, 256, 512
QK, RV = HEADS * DK, HEADS * DV
WIDTH = 31
PAD = WIDTH - 1
NG, NPG = 4, 8
NE = NG * NPG
FF = 512
NL = 2
EPS = 1e-6
BLK = 32
QW = D // 4
GRP = 8
NBLK = 72
BIG = 1.0e6
FAR = 1.0e30
SLOT = 4096
NSLOT = 6

C_ID, C_TRI, C_ONE, C_IOTA, C_MOD = 0, 128, 256, 384, 456
C_INV, C_QOFF, C_REV4, C_REV32, C_A, C_TOK = 584, 585, 586, 590, 622, 630
NCONST = 638
G_MIX, G_FFN, G_HEAD, B_PW1, B_DW, LN_G, LN_B, W_DW = 0, 16, 32, 48, 64, 72, 80, 88
NPAR = W_DW + KT * WIDTH

TWO_PI = 6.283185307179586
PI = 3.1415925
ROUND = 12582912.0
TURN = (6.28125, 0.0019350051879882812, 3.0199159819567e-07)


class Link:

    def __init__(self, eng, sem):
        self.eng, self.sem, self.n = eng, sem, 0

    def sent(self, ins):
        ins.then_inc(self.sem, 1)
        self.n = self.n + 1

    def wait(self):
        self.eng.wait_ge(self.sem, self.n)

    def done(self, ins):
        self.sent(ins)
        self.wait()


def program(nc, x_in, pos_in, const_in, decay_in, par_in, w_in, w_out, w_pw1, w_pw2, b_pw2,
            w_router, b_router, w_gate, w_up, w_down, g_final, out):
    with ExitStack() as ctx:
        def sb(name, shape, dt=F32):
            return ctx.enter_context(nc.sbuf_tensor(name, shape, dt))

        def sem(name):
            return ctx.enter_context(nc.semaphore(name))

        def sems(name, n):
            return [sem(f"{name}{i}") for i in range(n)]

        ps = ctx.enter_context(nc.psum_tensor("ps", [P, 8, 512], F32))

        ring = sb("ring", [P, NSLOT, SLOT])
        x = sb("x", [P, NT, D])
        hT = sb("hT", [P, KT, S])
        area_a = sb("area_a", [P, 4096])
        area_b = sb("area_b", [P, KT * (S + PAD)])
        area_c = sb("area_c", [P, 6144])
        trig = sb("trig", [P, 2, S])
        const = sb("const", [P, NCONST])
        par = sb("par", [P, NPAR])
        wr = sb("wr", [P, NL, KT, NG + NE])
        rows = sb("rows", [1, D + NL * (NG + NE)])
        small = sb("small", [P, 64])
        cum = sb("cum", [P, NE + 2], I32)
        idx = sb("idx", [P, 2, NBLK], I32)
        idx_g = sb("idx_g", [P, GRP], I32)
        idx_s = sb("idx_s", [P, GRP], I32)
        wts = sb("wts", [P, 2, NT])
        hg = sb("hg", [P, QW])
        hgT = sb("hgT", [P, KT, BLK])
        sg_e = sb("sg_e", [P, P])
        a_e = sb("a_e", [P, P])
        aT_e = sb("aT_e", [P, P])

        ident = const[:, C_ID:C_ID + P]
        tri = const[:, C_TRI:C_TRI + P]
        ones = const[:, C_ONE:C_ONE + P]
        eps = small[:, 0:1]
        ss = small[:, 4:8]
        rt = small[:, 8:12]
        rstd = small[:, 12:16]
        mv = small[:, 16:24]
        stats = small[:, 24:48]

        xn = area_a[:, :].rearrange("p (i d) -> p i d", i=NT)
        sT = area_a[:, 0:2048].rearrange("p (j s) -> p j s", j=NT)
        oT = area_a[:, 2048:4096].rearrange("p (f s) -> p f s", f=NT)
        v = area_b[:, 0:2048].rearrange("p (j s) -> p j s", j=NT)
        sg = area_b[:, 2048:4096].rearrange("p (j s) -> p j s", j=NT)
        uT = area_b[:, :].rearrange("p (c s) -> p c s", c=KT)
        qT = area_c[:, 0:1024].rearrange("p (d s) -> p d s", d=2)
        kT = area_c[:, 1024:2048].rearrange("p (d s) -> p d s", d=2)
        tmp = area_c[:, 2048:4096].rearrange("p (d s) -> p d s", d=4)
        decay = area_c[:, 4096:6144].rearrange("p (h s) -> p h s", h=HEADS)
        z = area_c[:, 0:4096].rearrange("p (c s) -> p c s", c=KT)
        sig = area_c[:, 4096:5120].rearrange("p (b s) -> p b s", b=2)
        ytile = [area_a[:, 0:2048], area_a[:, 2048:4096],
                 hT[:, 0:4, :].rearrange("p k s -> p (k s)"), hT[:, 4:8, :].rearrange("p k s -> p (k s)")]

        logits = area_b[:, 0:144].rearrange("p (i e) -> p i e", i=NT)
        le = area_b[:, 144:272].rearrange("p (i e) -> p i e", i=NT)
        eq = area_b[:, 272:400].rearrange("p (i e) -> p i e", i=NT)
        onehot = area_b[:, 400:656]
        before = area_b[:, 656:944]
        work = area_b[:, 944:1200].rearrange("p (j e) -> p j e", j=8)
        group_hot = area_b[:, 1200:1216].rearrange("p (i g) -> p i g", i=NT)
        pick, best, second, gate = (area_b[:, 1216 + 4 * n:1220 + 4 * n] for n in range(4))
        rank, base = area_b[:, 1232:1240], area_b[:, 1240:1248]
        ranki, blki = area_b[:, 1248:1256].bitcast(I32), area_b[:, 1256:1264].bitcast(I32)
        count, blocks, upto = area_b[:, 1264:1296].bitcast(I32), area_b[:, 1296:1328], area_b[:, 1328:1360]
        gfin = area_b[:, 1408:1408 + D]
        slot_hot = area_c[:, 0:1024].rearrange("p (j s) -> p j s", j=8)
        block_hot = area_c[:, 1024:1024 + 16 * NBLK].rearrange("p (j b) -> p j b", j=8)
        hg_in = area_a[:, 0:GRP * QW].rearrange("p (b c) -> p b c", b=GRP)
        y_out = area_c[:, 4096:4096 + GRP * QW].rearrange("p (b c) -> p b c", b=GRP)

        xn_dram = [nc.dram_tensor(f"xn_dram{l}", [4 * S, QW], F32, kind="Internal").ap() for l in range(NL)]
        y_dram = [nc.dram_tensor(f"y_dram{l}", [8 * S, QW], F32, kind="Internal").ap() for l in range(NL)]

        slot_loaded = sems("slot_loaded", NSLOT)
        x_loaded = sems("x_loaded", NT)
        const_loaded = sem("const_loaded")
        decay_loaded = sem("decay_loaded")
        par_loaded = sem("par_loaded")
        pos_loaded = sem("pos_loaded")
        gfin_loaded = sem("gfin_loaded")
        xn_stored = sems("xn_stored", NL)
        y_loaded = [sems(f"y_loaded{l}_", NT) for l in range(NL)]
        out_stored = sem("out_stored")
        dve_link = sem("dve_link")
        act_link = sem("act_link")
        pool_link = sem("pool_link")
        root_ready = sem("root_ready")
        xn_ready = sem("xn_ready")
        hT_mm = sem("hT_mm")
        hT_even = sem("hT_even")
        hT_odd = sem("hT_odd")
        combined = sem("combined")
        trig_arg = sem("trig_arg")
        trig_ready = sem("trig_ready")
        qk_mm, v_mm, sc_mm, g_mm, pv_mm, tr_mm, out_mm = (
            sem(n) for n in ("qk_mm", "v_mm", "sc_mm", "g_mm", "pv_mm", "tr_mm", "out_mm"))
        rot_ready, sT_ready, on_ready, x_added = (
            sem(n) for n in ("rot_ready", "sT_ready", "on_ready", "x_added"))
        v_ready, sg_ready, oroot_ready, oT_ready = (
            sem(n) for n in ("v_ready", "sg_ready", "oroot_ready", "oT_ready"))
        act_head, dve_head, dve_norm = sem("act_head"), sem("dve_head"), sem("dve_norm")
        pw1_mm, sig_ready, u_ready, z_ready, zt_mm, lnroot_ready, lnscale_ready, zn_ready, ztb_mm, zh_ready, \
            pw2_mm, x2_added, pad_zero, dve_conv = (
                sem(n) for n in ("pw1_mm", "sig_ready", "u_ready", "z_ready", "zt_mm", "lnroot_ready",
                                 "lnscale_ready", "zn_ready", "ztb_mm", "zh_ready", "pw2_mm", "x2_added",
                                 "pad_zero", "dve_conv"))
        def both(name):
            return sems(name, NL)
        logit_mm, exp_arg, exp_ready, onehot_ready, rank_mm, cum_ready, spread_ready, idx_mm, idx_ready = (
            both(n) for n in ("logit_mm", "exp_arg", "exp_ready", "onehot_ready", "rank_mm", "cum_ready",
                              "spread_ready", "idx_mm", "idx_ready"))
        gathered = [sems(f"gathered{l}_", GRP) for l in range(NL)]
        scattered_lo, scattered_hi, rows_in, staged, y_free, rows_out = (
            both(n) for n in ("scattered_lo", "scattered_hi", "rows_in", "staged", "y_free", "rows_out"))
        idx_copied, t1_mm, hgT_ready, gu_mm, silu_ready, act_ready, t2_mm, aT_ready, \
            y_mm, y_ready = (
                both(n) for n in ("idx_copied", "t1_mm", "hgT_ready", "gu_mm",
                                  "silu_ready", "act_ready", "t2_mm", "aT_ready", "y_mm", "y_ready"))

        after_ret = [128, 64, 64, 64, 0, 0]

        def expert_base(l, s):
            return after_ret[s] + l * (16 * NE // 2 + 16)

        slots_of = [(4, 5, 0), (1, 2, 3)]
        pw1_slot = {0: 4, 2: 5, 1: 0, 3: 1}
        pw2_slot = {0: 2, 1: 3}

        block = ctx.enter_context(nc.Block())

        @block.sync
        def _(sp):
            def load_columns(s, w, k, lo, n, at=0):
                dst = ring[:, s, 0:k * SLOT // k].rearrange("p (k c) -> p k c", k=k)[:, :, at:at + n]
                sp.dma_start(dst, w[:, bass.ds(lo, n)].rearrange("(k p) c -> p k c", p=P)) \
                    .then_inc(slot_loaded[s], 16)

            def load_rows(s, w, lo, n):
                k = n // P
                dst = ring[:, s, :].rearrange("p (k c) -> p k c", k=k)
                sp.dma_start(dst, w[bass.ds(lo, n), :].rearrange("(k p) c -> p k c", p=P)) \
                    .then_inc(slot_loaded[s], 16)

            def load_head_qk(h):
                load_columns(0, w_in, KT, h * DK, DK)
                load_columns(0, w_in, KT, h * DK + QK, DK, at=DK)

            for i in range(NT):
                sp.dma_start(x[:, i, :], x_in[i * P:(i + 1) * P, :]).then_inc(x_loaded[i], 16)
                if i == 0:
                    sp.dma_start(const[:, :], const_in).then_inc(const_loaded, 16)
            load_head_qk(0)
            sp.dma_start(decay[:, :, :], decay_in.rearrange("h p s -> p h s")).then_inc(decay_loaded, 16)
            load_columns(1, w_in, KT, 2 * QK, DV)
            load_columns(2, w_in, KT, 2 * QK + RV, DV)
            load_rows(3, w_out, 0, DV)
            load_rows(4, w_gate[0, 0], 0, D)
            load_rows(5, w_up[0, 0], 0, D)
            with sp.Fori(1, HEADS) as h:
                sp.wait_ge(qk_mm, 4 * h)
                load_head_qk(h)
                sp.wait_ge(v_mm, 4 * h)
                load_columns(1, w_in, KT, h * DV + 2 * QK, DV)
                sp.wait_ge(g_mm, 4 * h)
                load_columns(2, w_in, KT, h * DV + (2 * QK + RV), DV)
                sp.wait_ge(out_mm, 8 * h)
                load_rows(3, w_out, h * DV, DV)
            sp.wait_ge(qk_mm, 4 * HEADS)
            load_rows(0, w_down[0, 0], 0, FF)
            sp.wait_ge(v_mm, 4 * HEADS)
            load_rows(1, w_gate[0, 1], 0, D)
            sp.wait_ge(g_mm, 4 * HEADS)
            load_rows(2, w_up[0, 1], 0, D)
            sp.wait_ge(out_mm, 8 * HEADS)
            load_rows(3, w_down[0, 1], 0, FF)

            for l in range(NL):
                sp.wait_ge(xn_ready, 4 * (2 * l + 2))
                sp.dma_start(xn_dram[l].rearrange("(i p q) c -> p i (q c)", i=NT, q=4), xn[:, :, :]) \
                    .then_inc(xn_stored[l], 16)
                gate_l = w_gate[l].rearrange("e d f -> (e d) f")
                up_l = w_up[l].rearrange("e d f -> (e d) f")
                down_l = w_down[l].rearrange("e f d -> (e f) d")
                sp.wait_ge(cum_ready[l], 1)
                if l == 1:
                    sp.dma_start(gfin[:, :], g_final.partition_broadcast(P)).then_inc(gfin_loaded, 16)
                with sp.Fori(1, NE // 2) as pair:
                    for odd in range(2):
                        s_gate, s_up, s_down = slots_of[odd]
                        upto = sp.value_load(cum[0:1, bass.ds(2 * pair + (odd - 1), 1)], min_val=1, max_val=NBLK - 1)
                        e = 2 * pair + odd
                        sp.wait_ge(gu_mm[l], upto)
                        load_rows(s_gate, gate_l, e * D, D)
                        load_rows(s_up, up_l, e * D, D)
                        sp.wait_ge(y_mm[l], upto)
                        load_rows(s_down, down_l, e * FF, FF)
                total = sp.value_load(cum[0:1, NE:NE + 1], min_val=NE, max_val=NBLK - 1)
                last = sp.value_load(cum[0:1, NE - 1:NE], min_val=1, max_val=NBLK - 1)
                if l == 0:
                    sp.wait_ge(gu_mm[l], last)
                    load_columns(pw1_slot[0], w_pw1, KT, 0, 512)
                    load_columns(pw1_slot[2], w_pw1, KT, 1024, 512)
                    sp.wait_ge(y_mm[l], last)
                    load_columns(pw1_slot[1], w_pw1, KT, 512, 512)
                    sp.wait_ge(gu_mm[l], total)
                    load_columns(pw1_slot[3], w_pw1, KT, 1536, 512)
                    load_columns(pw2_slot[0], w_pw2, KT, 0, 512)
                    sp.wait_ge(y_mm[l], total)
                    load_columns(pw2_slot[1], w_pw2, KT, 512, 512)
                sp.wait_ge(rows_out[l], 1)
                for i in range(NT):
                    sp.dma_start(ytile[i], y_dram[l].rearrange("(t r) c -> t (r c)", r=8)[i * P:(i + 1) * P, :]) \
                        .then_inc(y_loaded[l][i], 16)
                if l == 0:
                    sp.wait_ge(pw1_mm, 8)
                    load_rows(4, w_gate[1, 0], 0, D)
                    load_rows(5, w_up[1, 0], 0, D)
                    sp.wait_ge(pw1_mm, 16)
                    load_rows(0, w_down[1, 0], 0, FF)
                    load_rows(1, w_gate[1, 1], 0, D)
                    sp.wait_ge(pw2_mm, 4)
                    load_rows(2, w_up[1, 1], 0, D)
                    sp.wait_ge(pw2_mm, 8)
                    load_rows(3, w_down[1, 1], 0, FF)
            for i in range(NT):
                sp.wait_ge(xn_ready, 4 * 4 + i + 1)
                sp.dma_start(out[i * P:(i + 1) * P, :], xn[:, i, :]).then_inc(out_stored, 16)
            sp.wait_ge(out_stored, 16 * NT)

        @block.gpsimd
        def _(pool):
            pool.dma_start(area_b[:, 0:S].bitcast(I32), pos_in.partition_broadcast(P)).then_inc(pos_loaded, 16)
            pool.dma_start(par[:, :], par_in).then_inc(par_loaded, 16)
            pool.dma_start(wr[:, :, :, :], w_router).then_inc(par_loaded, 16)
            pool.dma_start(rows[0:1, 0:D], b_pw2).then_inc(par_loaded, 16)
            pool.dma_start(rows[0:1, D:D + NL * (NG + NE)], b_router).then_inc(par_loaded, 16)
            gather_bound, scatter_bound = pool.to_reg(4 * S - 1), pool.to_reg(8 * S - 1)

            for l in range(NL):
                def gather(b):
                    pool.indirect_dma_start(
                        hg_in[:, b, :], None, xn_dram[l],
                        bass.IndirectOffsetOnAxis(ap=idx_g[:, b:b + 1].bitcast(U32), axis=0),
                        bounds_check=gather_bound, oob_is_err=False).then_inc(gathered[l][b], 16)

                def scatter(b):
                    pool.indirect_dma_start(
                        y_dram[l], bass.IndirectOffsetOnAxis(ap=idx_s[:, b:b + 1].bitcast(U32), axis=0),
                        y_out[:, b, :], None, bounds_check=scatter_bound, oob_is_err=False) \
                        .then_inc((scattered_lo if b < GRP // 2 else scattered_hi)[l], 16)

                pool.wait_ge(idx_ready[l], 1)
                pool.wait_ge(xn_stored[l], 16)
                pool.tensor_copy(idx_g[:, :], idx[:, 1, 0:GRP]).then_inc(idx_copied[l], 1)
                pool.wait_ge(idx_copied[l], 1)
                for b in range(GRP):
                    gather(b)
                pool.sem_inc(y_free[l], GRP)
                for b in range(GRP // 2):
                    pool.wait_ge(gathered[l][b], 16)
                    pool.sem_inc(rows_in[l], 1)
                total = pool.value_load(cum[0:1, NE:NE + 1], min_val=NE, max_val=NBLK - GRP)
                steps = pool.value_load(cum[0:1, NE + 1:NE + 2], min_val=NE // GRP, max_val=NBLK // GRP - 1)
                for b in range(GRP):
                    pool.wait_ge(gathered[l][b], 16)
                with pool.Fori(0, steps) as g:
                    pool.tensor_copy(idx_g[:, :], idx[:, 1, bass.ds(GRP * g + GRP, GRP)]).then_inc(idx_copied[l], 1)
                    pool.tensor_copy(idx_s[:, :], idx[:, 0, bass.ds(GRP * g, GRP)]).then_inc(idx_copied[l], 1)
                    pool.wait_ge(idx_copied[l], 2 * g + 3)
                    for b in range(GRP):
                        ahead = (b + GRP // 2) % GRP
                        pool.wait_ge(gathered[l][ahead], 16 * g + (16 if ahead > b else 32))
                        pool.sem_inc(rows_in[l], 1)
                        pool.wait_ge(staged[l], GRP * g + (b + 1))
                        pool.nop(nofuse=True)
                        gather(b)
                        pool.wait_ge(y_ready[l], GRP * g + (b + 1))
                        pool.nop(nofuse=True)
                        scatter(b)
                        if b == GRP - 2:
                            pool.wait_ge(scattered_lo[l], 8 * GRP * g + 8 * GRP)
                            pool.sem_inc(y_free[l], GRP // 2)
                    pool.wait_ge(scattered_hi[l], 8 * GRP * g + 8 * GRP)
                    pool.sem_inc(y_free[l], GRP // 2)
                    for b in range(GRP):
                        pool.wait_ge(gathered[l][b], 16 * g + 32)
                pool.wait_ge(staged[l], total + 2)
                pool.sem_inc(rows_out[l], 1)

        @block.scalar
        def _(act):
            link = Link(act, act_link)

            def norm_roots(n, x_ready):
                for i in range(NT):
                    x_ready(i)
                    link.done(nc.scalar.activation(xn[:, i, :], x[:, i, :], ACT.Square, accum_out=ss[:, i:i + 1]))
                    nc.scalar.activation(rt[:, i:i + 1], ss[:, i:i + 1], ACT.Sqrt, bias=eps,
                                         scale=1.0 / D).then_inc(root_ready, 1)

            def norm_turned(n, gain):
                for k in range(0, KT, 2):
                    act.wait_ge(hT_mm, KT * n + k + 1)
                    nc.scalar.activation(hT[:, k, :], ps[:, k, :], ACT.Copy,
                                         scale=par[:, gain + k:gain + k + 1]).then_inc(hT_even, 1)

            def expert_blocks(l):
                act.wait_ge(exp_arg[l], 1)
                nc.scalar.activation(small[:, 48:64], small[:, 48:64], ACT.Exp).then_inc(exp_ready[l], 1)
                act.wait_ge(exp_arg[l], 2)
                nc.scalar.activation(small[:, 48:52], small[:, 48:52], ACT.Exp).then_inc(exp_ready[l], 1)
                act.wait_ge(cum_ready[l], 1)
                total = act.value_load(cum[0:1, NE:NE + 1], min_val=NE, max_val=NBLK - 1)
                with act.Fori(0, total) as t:
                    act.wait_ge(gu_mm[l], t + 1)
                    nc.scalar.activation(sg_e[:, :], ps[:, 2, 0:P], ACT.Silu).then_inc(silu_ready[l], 1)
                    act.wait_ge(t2_mm[l], t + 1)
                    nc.scalar.copy(aT_e[:, :], ps[:, 3, 0:P]).then_inc(aT_ready[l], 1)
                    act.wait_ge(y_mm[l], t + 1)
                    act.wait_ge(y_free[l], t + 1)
                    nc.scalar.copy(area_c[:, bass.ds((t % GRP) * QW + 4096, QW)], ps[:, 4, 0:QW]) \
                        .then_inc(y_ready[l], 1)
                act.wait_ge(y_ready[l], total)
                act.sem_inc(y_ready[l], GRP)

            act.wait_ge(const_loaded, 16)
            act.wait_ge(par_loaded, 64)
            act.wait_ge(pad_zero, 1)
            norm_roots(0, lambda i: act.wait_ge(x_loaded[i], 16))
            norm_turned(0, G_MIX)
            act.wait_ge(trig_arg, 1)
            nc.scalar.activation(trig[:, :, :], trig[:, :, :], ACT.Sin).then_inc(trig_ready, 1)
            with act.Fori(0, HEADS) as h:
                for i in range(NT):
                    act.wait_ge(v_mm, 4 * h + (i + 1))
                    nc.scalar.copy(v[:, i, :], ps[:, 4 + i, :]).then_inc(v_ready, 1)
                for i in range(NT):
                    act.wait_ge(g_mm, 4 * h + (i + 1))
                    nc.scalar.activation(sg[:, i, :], ps[:, i, :], ACT.Silu).then_inc(sg_ready, 1)
                for i in range(NT):
                    act.wait_ge(pv_mm, 4 * h + (i + 1))
                    nc.scalar.activation(oT[:, i, :], ps[:, 4 + i, :], ACT.Square,
                                         accum_out=ss[:, i:i + 1]).then_inc(act_head, 1)
                    act.wait_ge(act_head, 4 * h + (i + 1))
                    nc.scalar.activation(rt[:, i:i + 1], ss[:, i:i + 1], ACT.Sqrt, bias=eps,
                                         scale=1.0 / DV).then_inc(oroot_ready, 1)
                for f in range(NT):
                    act.wait_ge(tr_mm, 4 * h + (f + 1))
                    nc.scalar.activation(oT[:, f, :], ps[:, f, :], ACT.Copy,
                                         scale=par[:, bass.ds(4 * h + (G_HEAD + f), 1)]).then_inc(oT_ready, 1)
                act.wait_ge(out_mm, 8 * h + 8)
            norm_roots(1, lambda i: act.wait_ge(x_added, 8 * (HEADS - 1) + 2 * (i + 1) if i < 2 else 8 * HEADS))
            norm_turned(1, G_FFN)
            expert_blocks(0)

            norm_roots(2, lambda i: act.wait_ge(combined, i + 1))
            norm_turned(2, G_MIX + KT)
            for c in range(KT):
                act.wait_ge(pw1_mm, 2 * c + 2)
                if c >= 2:
                    act.wait_ge(u_ready, c - 1)
                nc.scalar.activation(sig[:, c % 2, :], ps[:, 2 * (c % 4) + 1, :], ACT.Sigmoid,
                                     bias=par[:, B_PW1 + KT + c:B_PW1 + KT + c + 1]).then_inc(sig_ready, 1)
            for i in range(NT):
                act.wait_ge(lnroot_ready, 2 * i + 1)
                nc.scalar.activation(rt[:, i:i + 1], mv[:, 2 * i + 1:2 * i + 2], ACT.Sqrt,
                                     bias=eps).then_inc(lnscale_ready, 1)
                act.wait_ge(lnroot_ready, 2 * i + 2)
                nc.scalar.activation(xn[:, i, :], ps[:, 2 * i:2 * i + 2, :].rearrange("p b s -> p (b s)"),
                                     ACT.Identity, bias=ss[:, i:i + 1], scale=rstd[:, i:i + 1]) \
                    .then_inc(zn_ready, 1)
            for k in range(KT):
                act.wait_ge(ztb_mm, k + 1)
                nc.scalar.activation(hT[:, k, :], ps[:, k, :], ACT.Silu, bias=par[:, LN_B + k:LN_B + k + 1],
                                     scale=par[:, LN_G + k:LN_G + k + 1]).then_inc(zh_ready, 1)
            norm_roots(3, lambda i: act.wait_ge(x2_added, NT + i + 1))
            norm_turned(3, G_FFN + KT)
            expert_blocks(1)
            norm_roots(4, lambda i: act.wait_ge(combined, NT + i + 1))

        @block.tensor
        def _(pe):
            def turn_norm(n):
                for k in range(KT):
                    for i in range(NT):
                        if k == 0:
                            pe.wait_ge(xn_ready, 4 * n + i + 1)
                        last = nc.tensor.transpose(ps[:, k, i * P:(i + 1) * P], xn[:, i, k * P:(k + 1) * P], ident)
                    last.then_inc(hT_mm, 1)

            def wait_norm(n):
                pe.wait_ge(hT_even, 4 * (n + 1))
                pe.wait_ge(hT_odd, 4 * (n + 1))

            def route(l):
                for i in range(NT):
                    at = ps[:, 0, i * 64:i * 64 + NG + NE]
                    for k in range(KT):
                        nc.tensor.matmul(at, hT[:, k, i * P:(i + 1) * P], wr[:, l, k, :], start=(k == 0), stop=False)
                    last = nc.tensor.matmul(at, const[0:1, C_ONE:C_ONE + P],
                                            rows[0:1, D + l * (NG + NE):D + (l + 1) * (NG + NE)],
                                            start=False, stop=True)
                last.then_inc(logit_mm[l], 1)
                pe.wait_ge(onehot_ready[l], 1)
                nc.tensor.matmul(ps[:, 5, 0:8 * NE], tri, onehot[:, :], start=True, stop=False)
                nc.tensor.matmul(ps[:, 5, 0:8 * NE], ones, before[:, 0:8 * NE], start=False, stop=True)
                nc.tensor.matmul(ps[:, 6, 0:NE], ones, before[:, 8 * NE:9 * NE], start=True, stop=True) \
                    .then_inc(rank_mm[l], 1)
                pe.wait_ge(spread_ready[l], 1)
                for j in range(8):
                    last = nc.tensor.matmul(ps[:, 7, 0:2 * NBLK], slot_hot[:, j, :], block_hot[:, j, :],
                                            start=(j == 0), stop=(j == 7))
                last.then_inc(idx_mm[l], 1)

            def turn_block(l, t):
                pe.wait_ge(staged[l], t + 1)
                for c in range(2):
                    last = nc.tensor.transpose(ps[:, 1, c * P:(c + 1) * P], hg[:, c * P:(c + 1) * P], ident)
                last.then_inc(t1_mm[l], 1)

            def one_block(l, t, pair, s_gate, s_up, s_down):
                gate_up = ring[:, s_gate:s_gate + 2, :].rearrange("p w (k f) -> p w k f", k=KT)
                down = ring[:, s_down, :].rearrange("p (k d) -> p k d", k=4)
                pe.wait_ge(hgT_ready[l], t + 1)
                for s in (s_gate, s_up):
                    pe.wait_ge(slot_loaded[s], 16 * pair + (expert_base(l, s) + 16))
                for k in range(KT):
                    for g in range(4):
                        last = nc.tensor.matmul(ps[32 * g:32 * g + 32, 2, 0:256], hgT[:, k, :],
                                                gate_up[:, :, k, g * P:(g + 1) * P],
                                                start=(k == 0), stop=(k == KT - 1), tile_position=(0, 32 * g))
                last.then_inc(gu_mm[l], 1)
                turn_block(l, t + 1)
                pe.wait_ge(act_ready[l], t + 1)
                nc.tensor.transpose(ps[:, 3, 0:P], a_e[:, :], ident).then_inc(t2_mm[l], 1)
                pe.wait_ge(aT_ready[l], t + 1)
                pe.wait_ge(slot_loaded[s_down], 16 * pair + (expert_base(l, s_down) + 16))
                for k in range(4):
                    for g in range(4):
                        last = nc.tensor.matmul(ps[32 * g:32 * g + 32, 4, 0:256], aT_e[:, k * BLK:(k + 1) * BLK],
                                                down[:, k, g * 256:(g + 1) * 256],
                                                start=(k == 0), stop=(k == 3), tile_position=(0, 32 * g))
                last.then_inc(y_mm[l], 1)

            def experts(l):
                turn_block(l, 0)
                with pe.Fori(0, NE // 2) as pair:
                    for odd in range(2):
                        slots = slots_of[odd]
                        first = pe.value_load(cum[0:1, bass.ds(2 * pair + odd, 1)], min_val=0, max_val=NBLK - 2)
                        after = pe.value_load(cum[0:1, bass.ds(2 * pair + (odd + 1), 1)], min_val=1, max_val=NBLK - 1)
                        with pe.Fori(first, after) as t:
                            one_block(l, t, pair, *slots)

            pe.wait_ge(const_loaded, 16)
            turn_norm(0)
            wait_norm(0)
            with pe.Fori(0, HEADS) as h:
                pe.wait_ge(slot_loaded[0], 32 * h + 32)
                for m in range(4):
                    for k in range(KT):
                        last = nc.tensor.matmul(ps[:, m, :], ring[:, 0, k * 512 + m * P:k * 512 + (m + 1) * P],
                                                hT[:, k, :], start=(k == 0), stop=(k == KT - 1))
                    last.then_inc(qk_mm, 1)
                pe.wait_ge(slot_loaded[1], 16 * h + 16)
                for i in range(NT):
                    for k in range(KT):
                        last = nc.tensor.matmul(ps[:, 4 + i, :], hT[:, k, i * P:(i + 1) * P],
                                                ring[:, 1, k * 512:(k + 1) * 512], start=(k == 0), stop=(k == KT - 1))
                    last.then_inc(v_mm, 1)
                pe.wait_ge(rot_ready, 4 * h + 4)
                for j in range(NT):
                    pe.wait_ge(v_ready, 4 * h + (j + 1))
                    for d in range(2):
                        last = nc.tensor.matmul(ps[:, 4 + j, 0:S - j * P], kT[:, d, j * P:(j + 1) * P],
                                                qT[:, d, j * P:S], start=(d == 0), stop=(d == 1))
                    last.then_inc(sc_mm, 1)
                pe.wait_ge(slot_loaded[2], 16 * h + 16)
                for i in range(NT):
                    for k in range(KT):
                        last = nc.tensor.matmul(ps[:, i, :], hT[:, k, i * P:(i + 1) * P],
                                                ring[:, 2, k * 512:(k + 1) * 512], start=(k == 0), stop=(k == KT - 1))
                    last.then_inc(g_mm, 1)
                pe.wait_ge(sT_ready, 4 * h + 4)
                for i in range(NT):
                    for j in range(i + 1):
                        last = nc.tensor.matmul(ps[:, 4 + i, :], sT[:, j, i * P:(i + 1) * P], v[:, j, :],
                                                start=(j == 0), stop=(j == i))
                    last.then_inc(pv_mm, 1)
                pe.wait_ge(on_ready, 4 * h + 4)
                for f in range(NT):
                    for i in range(NT):
                        last = nc.tensor.transpose(ps[:, f, i * P:(i + 1) * P], sg[:, i, f * P:(f + 1) * P], ident)
                    last.then_inc(tr_mm, 1)
                pe.wait_ge(slot_loaded[3], 16 * h + 16)
                pe.wait_ge(oT_ready, 4 * h + 4)
                for m in range(8):
                    i, n = m // 2, m % 2
                    for f in range(4):
                        last = nc.tensor.matmul(ps[:, m, :], oT[:, f, i * P:(i + 1) * P],
                                                ring[:, 3, f * D + n * 512:f * D + (n + 1) * 512],
                                                start=(f == 0), stop=(f == 3))
                    last.then_inc(out_mm, 1)
                pe.wait_ge(x_added, 8 * h + 8)
            turn_norm(1)
            wait_norm(1)
            route(0)
            experts(0)

            turn_norm(2)
            wait_norm(2)
            for c in range(KT):
                for half in range(2):
                    chunk = 2 * half + c // 4
                    s = pw1_slot[chunk]
                    if c % 4 == 0:
                        pe.wait_ge(slot_loaded[s], expert_base(1, s))
                    bank = 2 * (c % 4) + half
                    if c >= 4 and half == 0:
                        pe.wait_ge(u_ready, c - 3)
                    for k in range(KT):
                        at = k * 512 + (c % 4) * P
                        last = nc.tensor.matmul(ps[:, bank, :], ring[:, s, at:at + P], hT[:, k, :],
                                                start=(k == 0), stop=(k == KT - 1))
                    last.then_inc(pw1_mm, 1)
            pe.wait_ge(u_ready, KT)
            for c in range(KT):
                pe.wait_ge(z_ready, c + 1)
                for i in range(NT):
                    last = nc.tensor.transpose(ps[:, 2 * i + c // 4, (c % 4) * P:(c % 4 + 1) * P],
                                               z[:, c, i * P:(i + 1) * P], ident)
            last.then_inc(zt_mm, 1)
            pe.wait_ge(zn_ready, NT)
            for k in range(KT):
                for i in range(NT):
                    last = nc.tensor.transpose(ps[:, k, i * P:(i + 1) * P], xn[:, i, k * P:(k + 1) * P], ident)
                last.then_inc(ztb_mm, 1)
            pe.wait_ge(zh_ready, KT)
            for n in range(2):
                s = pw2_slot[n]
                pe.wait_ge(slot_loaded[s], expert_base(1, s))
                for i in range(NT):
                    m = 2 * i + n
                    for k in range(KT):
                        nc.tensor.matmul(ps[:, m, :], hT[:, k, i * P:(i + 1) * P],
                                         ring[:, s, k * 512:(k + 1) * 512], start=(k == 0), stop=False)
                    nc.tensor.matmul(ps[:, m, :], const[0:1, C_ONE:C_ONE + P], rows[0:1, n * 512:(n + 1) * 512],
                                     start=False, stop=True).then_inc(pw2_mm, 1)
            turn_norm(3)
            wait_norm(3)
            route(1)
            experts(1)

        @block.vector
        def _(dve):
            link = Link(dve, dve_link)
            V = nc.vector

            def scale_norm(n):
                for i in range(NT):
                    dve.wait_ge(root_ready, 4 * n + i + 1)
                    link.done(V.reciprocal(rstd[:, i:i + 1], rt[:, i:i + 1]))
                    if n < 4:
                        V.tensor_scalar(xn[:, i, :], x[:, i, :], rstd[:, i:i + 1], None, ALU.mult) \
                            .then_inc(xn_ready, 1)
                    else:
                        V.scalar_tensor_tensor(out=xn[:, i, :], in0=x[:, i, :], scalar=rstd[:, i:i + 1],
                                               in1=gfin[:, :], op0=ALU.mult, op1=ALU.mult).then_inc(xn_ready, 1)

            def turned_norm(n, gain):
                for k in range(1, KT, 2):
                    dve.wait_ge(hT_mm, KT * n + k + 1)
                    V.tensor_scalar(hT[:, k, :], ps[:, k, :], par[:, gain + k:gain + k + 1], None, ALU.mult) \
                        .then_inc(hT_odd, 1)

            def first_max(l, scores, best, rev, n, oh):
                shape = [P, NT, n]
                link.done(V.tensor_tensor(eq[:, :, 0:n], scores, best.unsqueeze(2).to_broadcast(shape), ALU.is_equal))
                link.done(V.tensor_tensor(eq[:, :, 0:n], eq[:, :, 0:n], rev.unsqueeze(1).to_broadcast(shape), ALU.mult))
                link.done(V.tensor_reduce(pick[:, :], eq[:, :, 0:n], AX, ALU.max))
                link.done(V.tensor_tensor(oh, eq[:, :, 0:n], pick[:, :].unsqueeze(2).to_broadcast(shape), ALU.is_equal))

            def route(l):
                dve.wait_ge(logit_mm[l], 1)
                link.done(V.tensor_copy(logits[:, :, :], ps[:, 0, 0:256].rearrange("p (i e) -> p i e", i=NT)
                                        [:, :, 0:NG + NE]))
                lg = logits[:, :, 0:NG]
                link.done(V.tensor_reduce(best[:, :], lg, AX, ALU.max))
                V.tensor_tensor(small[:, 48:64].rearrange("p (i g) -> p i g", i=NT), lg,
                                best[:, :].unsqueeze(2).to_broadcast([P, NT, NG]), ALU.subtract) \
                    .then_inc(exp_arg[l], 1)
                first_max(l, lg, best[:, :], const[:, C_REV4:C_REV4 + NG], NG, group_hot[:, :, :])
                dve.wait_ge(exp_ready[l], 1)
                link.done(V.tensor_reduce(gate[:, :], small[:, 48:64].rearrange("p (i g) -> p i g", i=NT), AX, ALU.add))
                link.done(V.reciprocal(gate[:, :], gate[:, :]))
                link.done(V.tensor_scalar(group_hot[:, :, :], group_hot[:, :, :], -1.0, FAR, ALU.add, ALU.mult))
                for i in range(NT):
                    link.sent(V.tensor_tensor(
                        le[:, i, :].rearrange("p (g e) -> p g e", g=NG),
                        logits[:, i, NG:NG + NE].rearrange("p (g e) -> p g e", g=NG),
                        group_hot[:, i, :].unsqueeze(2).to_broadcast([P, NG, NPG]), ALU.add))
                link.wait()
                rev = const[:, C_REV32:C_REV32 + NE]
                oh = onehot[:, :].rearrange("p (j e) -> p j e", j=8)
                link.done(V.tensor_reduce(best[:, :], le[:, :, :], AX, ALU.max))
                first_max(l, le[:, :, :], best[:, :], rev, NE, oh[:, 0:NT, :])
                link.done(V.scalar_tensor_tensor(out=le[:, :, :], in0=oh[:, 0:NT, :], scalar=-3.0 * FAR,
                                                 in1=le[:, :, :], op0=ALU.mult, op1=ALU.add))
                link.done(V.tensor_reduce(second[:, :], le[:, :, :], AX, ALU.max))
                V.tensor_tensor(small[:, 48:52], second[:, :], best[:, :], ALU.subtract).then_inc(exp_arg[l], 1)
                first_max(l, le[:, :, :], second[:, :], rev, NE, oh[:, NT:2 * NT, :])
                link.done(V.memset(before[:, 0:NE], 0.0))
                for j in range(8):
                    ins = V.tensor_tensor(before[:, (j + 1) * NE:(j + 2) * NE], before[:, j * NE:(j + 1) * NE],
                                          onehot[:, j * NE:(j + 1) * NE], ALU.add)
                    if j < 7:
                        link.done(ins)
                ins.then_inc(onehot_ready[l], 1)
                dve.wait_ge(exp_ready[l], 2)
                link.done(V.tensor_scalar(second[:, :], small[:, 48:52], 1.0, None, ALU.add))
                link.done(V.reciprocal(second[:, :], second[:, :]))
                link.done(V.tensor_tensor(wts[:, 0, :], second[:, :], gate[:, :], ALU.mult))
                link.done(V.tensor_tensor(wts[:, 1, :], wts[:, 0, :], small[:, 48:52], ALU.mult))
                dve.wait_ge(rank_mm[l], 1)
                link.done(V.tensor_scalar(count[:, :], ps[:, 6, 0:NE], BLK - 1.0, None, ALU.add))
                link.done(V.tensor_single_scalar(count[:, :], count[:, :], 5, ALU.arith_shift_right))
                link.done(V.tensor_scalar(blocks[:, :], count[:, :], 1.0, None, ALU.max))
                link.done(V.tensor_tensor_scan(upto[:, :], blocks[:, :], blocks[:, :], 0.0, ALU.add, ALU.bypass))
                link.sent(V.tensor_copy(cum[:, 1:NE + 1], upto[:, :]))
                link.done(V.tensor_scalar(count[:, 0:1], upto[:, NE - 1:NE], GRP - 1.0, None, ALU.add))
                V.tensor_single_scalar(cum[:, NE + 1:NE + 2], count[:, 0:1], 3, ALU.arith_shift_right) \
                    .then_inc(cum_ready[l], 1)
                link.done(V.tensor_tensor(upto[:, :], upto[:, :], blocks[:, :], ALU.subtract))
                rank3 = ps[:, 5, 0:8 * NE].rearrange("p (j e) -> p j e", j=8)
                link.done(V.tensor_tensor(work[:, :, :], rank3, oh, ALU.mult))
                link.done(V.tensor_reduce(rank[:, :], work[:, :, :], AX, ALU.add))
                link.done(V.tensor_tensor(work[:, :, :], oh, upto[:, :].unsqueeze(1).to_broadcast([P, 8, NE]), ALU.mult))
                link.done(V.tensor_reduce(base[:, :], work[:, :, :], AX, ALU.add))
                link.done(V.tensor_copy(ranki[:, :], rank[:, :]))
                link.done(V.tensor_single_scalar(blki[:, :], ranki[:, :], 5, ALU.arith_shift_right))
                link.done(V.tensor_single_scalar(ranki[:, :], ranki[:, :], BLK - 1, ALU.bitwise_and))
                link.done(V.tensor_copy(rank[:, :], ranki[:, :]))
                link.done(V.tensor_tensor(base[:, :], base[:, :], blki[:, :], ALU.add))
                link.sent(V.tensor_tensor(slot_hot[:, :, :],
                                          const[:, C_MOD:C_MOD + P].unsqueeze(1).to_broadcast([P, 8, P]),
                                          rank[:, :].unsqueeze(2).to_broadcast([P, 8, P]), ALU.is_equal))
                link.done(V.tensor_tensor(block_hot[:, :, 0:NBLK],
                                          const[:, C_IOTA:C_IOTA + NBLK].unsqueeze(1).to_broadcast([P, 8, NBLK]),
                                          base[:, :].unsqueeze(2).to_broadcast([P, 8, NBLK]), ALU.is_equal))
                link.done(V.tensor_tensor(block_hot[:, :, NBLK:2 * NBLK], block_hot[:, :, 0:NBLK],
                                          const[:, C_TOK:C_TOK + 8].unsqueeze(2).to_broadcast([P, 8, NBLK]), ALU.mult))
                V.tensor_tensor(block_hot[:, :, 0:NBLK], block_hot[:, :, 0:NBLK],
                                const[:, C_A:C_A + 8].unsqueeze(2).to_broadcast([P, 8, NBLK]), ALU.mult) \
                    .then_inc(spread_ready[l], 1)
                dve.wait_ge(idx_mm[l], 1)
                dve.wait_ge(spread_ready[l], 1)
                table = before[:, 0:2 * NBLK]
                link.done(V.tensor_scalar(table, ps[:, 7, 0:2 * NBLK], 0.0, BIG, ALU.is_equal, ALU.mult))
                link.done(V.tensor_tensor(table, table, ps[:, 7, 0:2 * NBLK], ALU.add))
                V.tensor_scalar(idx[:, :, :], table.rearrange("p (a b) -> p a b", a=2), 4.0, const[:, C_QOFF:C_QOFF + 1],
                                ALU.mult, ALU.add).then_inc(idx_ready[l], 1)

            def turned_block(l, t, gain):
                for c in range(2):
                    ins = V.tensor_tensor(
                        hgT[:, :, :].rearrange("p (q c) s -> p c q s", c=2)[:, c],
                        ps[:, 1, c * P:(c + 1) * P].rearrange("p (q s) -> p q s", q=4),
                        par[:, gain:gain + KT].rearrange("p (q c) -> p c q", c=2)[:, c].unsqueeze(2)
                        .to_broadcast([P, 4, BLK]), ALU.mult)
                ins.then_inc(hgT_ready[l], 1)

            def stage(l, t):
                dve.wait_ge(rows_in[l], t + 1)
                V.tensor_copy(hg[:, :], area_a[:, bass.ds((t % GRP) * QW, QW)]).then_inc(staged[l], 1)

            def expert_blocks(l):
                gain = G_FFN + KT * l
                total = dve.value_load(cum[0:1, NE:NE + 1], min_val=NE, max_val=NBLK - 1)
                stage(l, 0)
                dve.wait_ge(t1_mm[l], 1)
                turned_block(l, 0, gain)
                stage(l, 1)
                with dve.Fori(0, total) as t:
                    dve.wait_ge(silu_ready[l], t + 1)
                    V.tensor_tensor(a_e[:, :], sg_e[:, :], ps[:, 2, P:2 * P], ALU.mult).then_inc(act_ready[l], 1)
                    dve.wait_ge(t1_mm[l], t + 2)
                    dve.wait_ge(gu_mm[l], t + 1)
                    turned_block(l, t + 1, gain)
                    stage(l, t + 2)
                dve.wait_ge(staged[l], total + 2)
                dve.sem_inc(staged[l], GRP)

            def combine(l):
                for i in range(NT):
                    dve.wait_ge(y_loaded[l][i], 16)
                    for k in range(2):
                        ins = V.scalar_tensor_tensor(out=x[:, i, :], in0=ytile[i][:, k * D:(k + 1) * D],
                                                     scalar=wts[:, k, i:i + 1], in1=x[:, i, :],
                                                     op0=ALU.mult, op1=ALU.add)
                        if k == 0:
                            link.done(ins)
                    ins.then_inc(combined, 1)

            V.memset(small[:, 0:4], EPS).then_inc(pad_zero, 1)
            link.done(V.memset(cum[:, 0:1], 0))
            dve.wait_ge(const_loaded, 16)
            dve.wait_ge(pos_loaded, 16)
            ang, turns, low, wrap = (tmp[:, n, :] for n in range(4))
            sin, cos = trig[:, 0, :], trig[:, 1, :]
            link.done(V.tensor_copy(ang, area_b[:, 0:S].bitcast(I32)))
            link.done(V.tensor_scalar(ang, ang, const[:, C_INV:C_INV + 1], None, ALU.mult))
            link.done(V.tensor_scalar(turns, ang, 1.0 / TWO_PI, ROUND, ALU.mult, ALU.add))
            link.done(V.tensor_scalar(turns, turns, ROUND, None, ALU.subtract))
            for part in TURN:
                link.done(V.scalar_tensor_tensor(out=ang, in0=turns, scalar=-part, in1=ang, op0=ALU.mult, op1=ALU.add))
            link.done(V.tensor_scalar(low, ang, TWO_PI / 4, None, ALU.add))
            link.done(V.tensor_scalar(wrap, low, PI, -TWO_PI, ALU.is_gt, ALU.mult))
            link.done(V.tensor_tensor(low, low, wrap, ALU.add))
            link.done(V.tensor_scalar(sin, ang, PI, -PI, ALU.min, ALU.max))
            V.tensor_scalar(cos, low, PI, -PI, ALU.min, ALU.max).then_inc(trig_arg, 1)
            dve.wait_ge(par_loaded, 64)
            scale_norm(0)
            turned_norm(0, G_MIX)
            dve.wait_ge(trig_ready, 1)
            dve.wait_ge(decay_loaded, 16)
            with dve.Fori(0, HEADS) as h:
                for n, dst in enumerate((qT, kT)):
                    lo, hi = ps[:, 2 * n, :], ps[:, 2 * n + 1, :]
                    dve.wait_ge(qk_mm, 4 * h + (2 * n + 2))
                    if n == 1:
                        dve.wait_ge(rot_ready, 4 * h + 2)
                    V.tensor_tensor(tmp[:, 0, :], lo, cos, ALU.mult)
                    V.tensor_tensor(tmp[:, 1, :], hi, sin, ALU.mult)
                    V.tensor_tensor(tmp[:, 2, :], lo, sin, ALU.mult)
                    V.tensor_tensor(tmp[:, 3, :], hi, cos, ALU.mult).then_inc(dve_head, 1)
                    dve.wait_ge(dve_head, 2 * h + (n + 1))
                    V.tensor_tensor(dst[:, 0, :], tmp[:, 0, :], tmp[:, 1, :], ALU.subtract).then_inc(rot_ready, 1)
                    V.tensor_tensor(dst[:, 1, :], tmp[:, 2, :], tmp[:, 3, :], ALU.add).then_inc(rot_ready, 1)
                for j in range(NT):
                    dve.wait_ge(sc_mm, 4 * h + (j + 1))
                    V.tensor_tensor(sT[:, j, j * P:S], ps[:, 4 + j, 0:S - j * P],
                                    decay[:, bass.ds(h, 1), 0:S - j * P].rearrange("p a s -> p (a s)"),
                                    ALU.mult).then_inc(sT_ready, 1)
                for i in range(NT):
                    dve.wait_ge(oroot_ready, 4 * h + (i + 1))
                    V.reciprocal(rstd[:, i:i + 1], rt[:, i:i + 1]).then_inc(dve_norm, 1)
                    dve.wait_ge(dve_norm, 4 * h + (i + 1))
                    dve.wait_ge(sg_ready, 4 * h + (i + 1))
                    V.scalar_tensor_tensor(out=sg[:, i, :], in0=ps[:, 4 + i, :], scalar=rstd[:, i:i + 1],
                                           in1=sg[:, i, :], op0=ALU.mult, op1=ALU.mult).then_inc(on_ready, 1)
                for m in range(8):
                    i, n = m // 2, m % 2
                    dve.wait_ge(out_mm, 8 * h + (m + 1))
                    V.tensor_tensor(x[:, i, n * 512:(n + 1) * 512], x[:, i, n * 512:(n + 1) * 512], ps[:, m, :],
                                    ALU.add).then_inc(x_added, 1)
            dve.wait_ge(x_added, 8 * HEADS)
            scale_norm(1)
            turned_norm(1, G_FFN)
            route(0)
            expert_blocks(0)
            combine(0)

            scale_norm(2)
            turned_norm(2, G_MIX + KT)
            link.done(V.memset(uT[:, :, 0:PAD], 0.0))
            for pair in range(KT // 2):
                for c in (2 * pair, 2 * pair + 1):
                    dve.wait_ge(sig_ready, c + 1)
                    V.scalar_tensor_tensor(out=uT[:, c, PAD:PAD + S], in0=ps[:, 2 * (c % 4), :],
                                           scalar=par[:, B_PW1 + c:B_PW1 + c + 1], in1=sig[:, c % 2, :],
                                           op0=ALU.add, op1=ALU.mult).then_inc(u_ready, 1)
                dve.wait_ge(u_ready, 2 * pair + 2)
                for k in range(WIDTH):
                    for c in (2 * pair, 2 * pair + 1):
                        tap = par[:, W_DW + c * WIDTH + k:W_DW + c * WIDTH + k + 1]
                        if k == 0:
                            ins = V.tensor_scalar(z[:, c, :], uT[:, c, 0:S], tap, par[:, B_DW + c:B_DW + c + 1],
                                                  ALU.mult, ALU.add)
                        else:
                            dve.wait_ge(dve_conv, 2 * (pair * (WIDTH - 1) + k - 1) + c % 2 + 1)
                            ins = V.scalar_tensor_tensor(out=z[:, c, :], in0=uT[:, c, k:k + S], scalar=tap,
                                                         in1=z[:, c, :], op0=ALU.mult, op1=ALU.add)
                        ins.then_inc(dve_conv if k < WIDTH - 1 else z_ready, 1)
            dve.wait_ge(zt_mm, 1)
            for i in range(NT):
                st = stats[:, 12 * (i % 2):12 * (i % 2) + 12]
                for b in range(2):
                    link.sent(V.bn_stats(st[:, 6 * b:6 * b + 6], ps[:, 2 * i + b, :]))
                link.wait()
                V.bn_aggr(mv[:, 2 * i:2 * i + 2], st).then_inc(lnroot_ready, 1)
                dve.wait_ge(lnscale_ready, i + 1)
                link.done(V.reciprocal(rstd[:, i:i + 1], rt[:, i:i + 1]))
                V.scalar_tensor_tensor(out=ss[:, i:i + 1], in0=mv[:, 2 * i:2 * i + 1], scalar=-1.0,
                                       in1=rstd[:, i:i + 1], op0=ALU.mult, op1=ALU.mult).then_inc(lnroot_ready, 1)
            for n in range(2):
                for i in range(NT):
                    dve.wait_ge(pw2_mm, 4 * n + i + 1)
                    V.tensor_tensor(x[:, i, n * 512:(n + 1) * 512], x[:, i, n * 512:(n + 1) * 512],
                                    ps[:, 2 * i + n, :], ALU.add).then_inc(x2_added, 1)
            scale_norm(3)
            turned_norm(3, G_FFN + KT)
            route(1)
            expert_blocks(1)
            combine(1)
            dve.wait_ge(gfin_loaded, 16)
            scale_norm(4)


_NAMES = ("x_in", "pos_in", "const_in", "decay_in", "par_in", "w_in", "w_out", "w_pw1", "w_pw2", "b_pw2",
          "w_router", "b_router", "w_gate", "w_up", "w_down", "g_final")


def shape_constants():
    c = np.zeros((P, NCONST), np.float32)
    p = np.arange(P)
    c[:, C_ID:C_ID + P] = np.eye(P)
    c[:, C_TRI:C_TRI + P] = p[:, None] < p[None, :]
    c[:, C_ONE:C_ONE + P] = 1.0
    c[:, C_IOTA:C_IOTA + NBLK] = np.arange(NBLK)
    c[:, C_MOD:C_MOD + P] = p % BLK
    c[:, C_INV] = np.float32(10000.0) ** (-np.arange(P, dtype=np.float32) / np.float32(P))
    c[:, C_QOFF] = p // BLK - 4
    c[:, C_REV4:C_REV4 + NG] = NG - np.arange(NG)
    c[:, C_REV32:C_REV32 + NE] = NE - np.arange(NE)
    for j in range(8):
        tok = (j % NT) * P + p
        c[:, C_A + j] = 2 * tok + j // NT + 1
        c[:, C_TOK + j] = tok + 1
    gap = np.arange(S)[None, :] - p[:, None]
    decay = np.zeros((HEADS, P, S), np.float64)
    for h in range(HEADS):
        decay[h] = np.where(gap >= 0, (1.0 - 2.0 ** (-5.0 - h)) ** np.maximum(gap, 0), 0.0) * DK ** -0.5
    return c, decay.astype(np.float32)


def kernel(**inputs):
    import concourse.bacc as bacc
    from concourse.bass_utils import run_bass_kernel_spmd

    a = {k: np.asarray(v) for k, v in inputs.items()}
    const, decay = shape_constants()

    def columns(w):
        return w.reshape(-1, P).T

    taps = a["conv_w_dw"][0].reshape(WIDTH, KT, P).transpose(2, 1, 0).reshape(P, KT * WIDTH)
    par = np.concatenate([columns(a["norm_mix_g"]), columns(a["norm_ffn_g"]), columns(a["ret_head_g"]),
                          columns(a["conv_b_pw1"]), columns(a["conv_b_dw"]), columns(a["conv_ln_g"]),
                          columns(a["conv_ln_b"]), taps], axis=1)
    router = np.concatenate([a["moe_w_rg"], a["moe_w_re"]], axis=2).reshape(NL, KT, P, NG + NE)
    arrays = {
        "x_in": a["x"][0], "pos_in": a["positions"], "const_in": const, "decay_in": decay, "par_in": par,
        "w_in": a["ret_w_in"][0], "w_out": a["ret_w_out"][0], "w_pw1": a["conv_w_pw1"][0],
        "w_pw2": a["conv_w_pw2"][0], "b_pw2": a["conv_b_pw2"], "w_router": router.transpose(2, 0, 1, 3),
        "b_router": np.concatenate([a["moe_b_rg"], a["moe_b_re"]], axis=1).reshape(1, NL * (NG + NE)),
        "w_gate": a["moe_w_gate"], "w_up": a["moe_w_up"], "w_down": a["moe_w_down"],
        "g_final": a["final_norm_g"].reshape(1, D),
    }
    arrays = {k: np.ascontiguousarray(v) for k, v in arrays.items()}
    nc = bacc.Bacc("TRN2", target_bir_lowering=False, num_devices=1)
    aps = [nc.dram_tensor(n, arrays[n].shape, mybir.dt.from_np(arrays[n].dtype), kind="ExternalInput").ap()
           for n in _NAMES]
    out = nc.dram_tensor("out", (S, D), F32, kind="ExternalOutput").ap()
    program(nc, *aps, out)
    r = run_bass_kernel_spmd(nc, [arrays], core_ids=[0])
    return np.asarray(r.results[0]["out"]).reshape(1, S, D)
```

```python
from contextlib import ExitStack

import numpy as np
import concourse.bass as bass
from concourse import mybir

ALU = mybir.AluOpType
ACT = mybir.ActivationFunctionType
F32 = mybir.dt.float32
F32R = mybir.dt.float32r
I32 = mybir.dt.int32
U32 = mybir.dt.uint32
AX = mybir.AxisListType.X

P = 128
S = 512
D = 1024
NT = S // P
KT = D // P
HEADS, DK, DV = 4, 256, 512
QK, RV = HEADS * DK, HEADS * DV
WIDTH = 31
PAD = WIDTH - 1
NG, NPG = 4, 8
NE = NG * NPG
FF = 512
NL = 2
EPS = 1e-6
BLK = 32
QW = D // 4
GRP = 8
NBLK = 72
BIG = 1.0e6
FAR = 1.0e30
SLOT = 4096
NSLOT = 6
NWT = 4
TILES = 8

C_ID, C_TRI, C_ONE, C_IOTA, C_MOD = 0, 128, 256, 384, 456
C_INV, C_QOFF, C_REV4, C_REV32, C_A, C_TOK = 584, 585, 586, 590, 622, 630
NCONST = 638
G_MIX, G_FFN, G_HEAD, B_PW1, B_DW, LN_G, LN_B, W_DW = 0, 16, 32, 48, 64, 72, 80, 88
NPAR = W_DW + KT * WIDTH

PE_CHANNELS = (2, 3)
DVE_CHANNELS = (0, 1, 4, 5, 6, 7)

TWO_PI = 6.283185307179586
PI = 3.1415925
ROUND = 12582912.0
TURN = (6.28125, 0.0019350051879882812, 3.0199159819567e-07)


class Link:

    def __init__(self, eng, sem):
        self.eng, self.sem, self.n = eng, sem, 0

    def sent(self, ins):
        ins.then_inc(self.sem, 1)
        self.n = self.n + 1

    def wait(self):
        self.eng.wait_ge(self.sem, self.n)

    def done(self, ins):
        self.sent(ins)
        self.wait()


def program(nc, x_in, pos_in, const_in, decay_in, par_in, w_in, w_out, w_pw1, w_pw2, b_pw2,
            w_router, b_router, w_gate, w_up, w_down, g_final, out):
    with ExitStack() as ctx:
        def sb(name, shape, dt=F32):
            return ctx.enter_context(nc.sbuf_tensor(name, shape, dt))

        def sem(name):
            return ctx.enter_context(nc.semaphore(name))

        def sems(name, n):
            return [sem(f"{name}{i}") for i in range(n)]

        def next_tensor():
            return -(-nc.sbuf_base // 32) * 32

        ps = ctx.enter_context(nc.psum_tensor("ps", [P, 8, 512], F32))

        ring_at = next_tensor()
        ring = sb("ring", [P, NSLOT, SLOT])
        x = sb("x", [P, NT, D])
        hT_at = next_tensor()
        hT = sb("hT", [P, KT, S])
        area_a_at = next_tensor()
        area_a = sb("area_a", [P, 4096])
        area_b = sb("area_b", [P, KT * (S + PAD)])
        area_c_at = next_tensor()
        area_c = sb("area_c", [P, 6144])
        trig = sb("trig", [P, 2, S])
        const = sb("const", [P, NCONST])
        par = sb("par", [P, NPAR])
        wr = sb("wr", [P, NL, KT, NG + NE])
        rows = sb("rows", [1, D + NL * (NG + NE)])
        small = sb("small", [P, 64])
        cum = sb("cum", [P, NE + 2], I32)
        idx = sb("idx", [P, 2, NBLK], I32)
        idx_g = sb("idx_g", [P, GRP], I32)
        idx_s = sb("idx_s", [P, GRP], I32)
        wts = sb("wts", [P, 2, NT])
        hg = sb("hg", [P, QW])
        hgT = sb("hgT", [P, KT, BLK])
        sg_e = sb("sg_e", [P, P])
        a_e = sb("a_e", [P, P])
        aT_e = sb("aT_e", [P, P])

        def over(name, shape, under, words):
            return nc.alloc_sbuf_tensor_at(name, shape, F32R, offset=under + 4 * words)

        hT_hi = over("hT_hi", [P, KT, S], hT_at, 0)
        w_hi = over("w_hi", [P, NWT, 512], ring_at, 4 * SLOT)
        w_lo = over("w_lo", [P, NWT, 512], ring_at, 4 * SLOT + NWT * 512)
        hT_lo = over("hT_lo", [P, KT, S], ring_at, 5 * SLOT)
        oT_hi = over("oT_hi", [P, NT, S], area_a_at, 2048)
        oT_lo = over("oT_lo", [P, NT, S], area_c_at, 2048)

        ident = const[:, C_ID:C_ID + P]
        tri = const[:, C_TRI:C_TRI + P]
        ones = const[:, C_ONE:C_ONE + P]
        eps = small[:, 0:1]
        ss = small[:, 4:8]
        rt = small[:, 8:12]
        rstd = small[:, 12:16]
        mv = small[:, 16:24]
        stats = small[:, 24:48]

        xn = area_a[:, :].rearrange("p (i d) -> p i d", i=NT)
        sT = area_a[:, 0:2048].rearrange("p (j s) -> p j s", j=NT)
        squares = area_a[:, 2048:4096].rearrange("p (f s) -> p f s", f=NT)
        diag = area_a[:, 0:8 * P].rearrange("p (b c) -> p b c", b=8)
        v = area_b[:, 0:2048].rearrange("p (j s) -> p j s", j=NT)
        sg = area_b[:, 2048:4096].rearrange("p (j s) -> p j s", j=NT)
        uT = area_b[:, :].rearrange("p (c s) -> p c s", c=KT)
        qT = area_c[:, 0:1024].rearrange("p (d s) -> p d s", d=2)
        kT = area_c[:, 1024:2048].rearrange("p (d s) -> p d s", d=2)
        tmp = area_c[:, 2048:4096].rearrange("p (d s) -> p d s", d=4)
        decay = area_c[:, 4096:6144].rearrange("p (h s) -> p h s", h=HEADS)
        z = area_c[:, 0:4096].rearrange("p (c s) -> p c s", c=KT)
        sig = area_c[:, 4096:5120].rearrange("p (b s) -> p b s", b=2)
        ytile = [area_a[:, 0:2048], area_a[:, 2048:4096],
                 hT[:, 0:4, :].rearrange("p k s -> p (k s)"), hT[:, 4:8, :].rearrange("p k s -> p (k s)")]

        logits = area_b[:, 0:144].rearrange("p (i e) -> p i e", i=NT)
        le = area_b[:, 144:272].rearrange("p (i e) -> p i e", i=NT)
        eq = area_b[:, 272:400].rearrange("p (i e) -> p i e", i=NT)
        onehot = area_b[:, 400:656]
        before = area_b[:, 656:944]
        work = area_b[:, 944:1200].rearrange("p (j e) -> p j e", j=8)
        group_hot = area_b[:, 1200:1216].rearrange("p (i g) -> p i g", i=NT)
        pick, best, second, gate = (area_b[:, 1216 + 4 * n:1220 + 4 * n] for n in range(4))
        rank, base = area_b[:, 1232:1240], area_b[:, 1240:1248]
        ranki, blki = area_b[:, 1248:1256].bitcast(I32), area_b[:, 1256:1264].bitcast(I32)
        count, blocks, upto = area_b[:, 1264:1296].bitcast(I32), area_b[:, 1296:1328], area_b[:, 1328:1360]
        gfin = area_b[:, 1408:1408 + D]
        slot_hot = area_c[:, 0:1024].rearrange("p (j s) -> p j s", j=8)
        block_hot = area_c[:, 1024:1024 + 16 * NBLK].rearrange("p (j b) -> p j b", j=8)
        hg_in = area_a[:, 0:GRP * QW].rearrange("p (b c) -> p b c", b=GRP)
        y_out = area_c[:, 4096:4096 + GRP * QW].rearrange("p (b c) -> p b c", b=GRP)

        xn_dram = [nc.dram_tensor(f"xn_dram{l}", [4 * S, QW], F32, kind="Internal").ap() for l in range(NL)]
        y_dram = [nc.dram_tensor(f"y_dram{l}", [8 * S, QW], F32, kind="Internal").ap() for l in range(NL)]

        slot_loaded = sems("slot_loaded", NSLOT)
        x_loaded = sems("x_loaded", NT)
        const_loaded = sem("const_loaded")
        decay_loaded = sem("decay_loaded")
        par_loaded = sem("par_loaded")
        pos_loaded = sem("pos_loaded")
        gfin_loaded = sem("gfin_loaded")
        xn_stored = sems("xn_stored", NL)
        y_loaded = [sems(f"y_loaded{l}_", NT) for l in range(NL)]
        out_stored = sem("out_stored")
        dve_link = sem("dve_link")
        act_link = sem("act_link")
        pool_link = sem("pool_link")
        root_ready = sem("root_ready")
        xn_ready = sem("xn_ready")
        hT_mm = sem("hT_mm")
        hT_even = sem("hT_even")
        hT_odd = sem("hT_odd")
        hi_ready, lo_ready, tile_used = sem("hi_ready"), sem("lo_ready"), sem("tile_used")
        hThi_ready, hTlo_ready, oTlo_ready = sem("hThi_ready"), sem("hTlo_ready"), sem("oTlo_ready")
        combined = sem("combined")
        trig_arg = sem("trig_arg")
        trig_ready = sem("trig_ready")
        sc_mm, pv_mm, tr_mm = (sem(n) for n in ("sc_mm", "pv_mm", "tr_mm"))
        rot_ready, sT_ready, on_ready, x_added = (
            sem(n) for n in ("rot_ready", "sT_ready", "on_ready", "x_added"))
        v_ready, sg_ready, oroot_ready, oT_ready = (
            sem(n) for n in ("v_ready", "sg_ready", "oroot_ready", "oT_ready"))
        act_head, dve_head, dve_norm = sem("act_head"), sem("dve_head"), sem("dve_norm")
        diag_ready, diag_used, zpe_ready = (sem(n) for n in ("diag_ready", "diag_used", "zpe_ready"))
        sig_ready, u_ready, z_ready, zt_mm, lnroot_ready, lnscale_ready, zn_ready, ztb_mm, zh_ready, \
            pw2_mm, x2_added, pad_zero, dve_conv = (
                sem(n) for n in ("sig_ready", "u_ready", "z_ready", "zt_mm", "lnroot_ready",
                                 "lnscale_ready", "zn_ready", "ztb_mm", "zh_ready", "pw2_mm", "x2_added",
                                 "pad_zero", "dve_conv"))
        def both(name):
            return sems(name, NL)
        logit_mm, exp_arg, exp_ready, onehot_ready, rank_mm, cum_ready, spread_ready, idx_mm, idx_ready = (
            both(n) for n in ("logit_mm", "exp_arg", "exp_ready", "onehot_ready", "rank_mm", "cum_ready",
                              "spread_ready", "idx_mm", "idx_ready"))
        gathered = [sems(f"gathered{l}_", GRP) for l in range(NL)]
        scattered_lo, scattered_hi, rows_in, staged, y_free, rows_out = (
            both(n) for n in ("scattered_lo", "scattered_hi", "rows_in", "staged", "y_free", "rows_out"))
        idx_copied, t1_mm, hgT_ready, gu_mm, silu_ready, act_ready, t2_mm, aT_ready, \
            y_mm, y_ready = (
                both(n) for n in ("idx_copied", "t1_mm", "hgT_ready", "gu_mm",
                                  "silu_ready", "act_ready", "t2_mm", "aT_ready", "y_mm", "y_ready"))

        after_ret = [128, 64, 64, 64, 0, 0]

        def expert_base(l, s):
            return after_ret[s] + l * (16 * NE // 2 + in_conv[s])

        slots_of = [(0, 1, 2), (3, 4, 5)]
        in_conv = [48, 48, 32, 32, 0, 0]
        ret_tiles = HEADS * 4 * TILES
        pw1_tiles = 4 * TILES

        def tile_column(output, k):
            return (k % 4) * D + (k // 4) * 512 if output else k * 512

        block = ctx.enter_context(nc.Block())

        @block.sync
        def _(sp):
            def load_columns(s, w, k, lo, n, at=0):
                dst = ring[:, s, :].rearrange("p (k c) -> p k c", k=k)[:, :, at:at + n]
                sp.dma_start(dst, w[:, bass.ds(lo, n)].rearrange("(k p) c -> p k c", p=P)) \
                    .then_inc(slot_loaded[s], 16)

            def load_rows(s, w, lo, n):
                k = n // P
                dst = ring[:, s, :].rearrange("p (k c) -> p k c", k=k)
                sp.dma_start(dst, w[bass.ds(lo, n), :].rearrange("(k p) c -> p k c", p=P)) \
                    .then_inc(slot_loaded[s], 16)

            def load_head_qk(h):
                load_columns(0, w_in, KT, h * DK, DK)
                load_columns(0, w_in, KT, h * DK + QK, DK, at=DK)

            for i in range(NT):
                sp.dma_start(x[:, i, :], x_in[i * P:(i + 1) * P, :]).then_inc(x_loaded[i], 16)
            load_head_qk(0)
            load_columns(1, w_in, KT, 2 * QK, DV)
            sp.dma_start(decay[:, :, :], decay_in.rearrange("h p s -> p h s")).then_inc(decay_loaded, 16)
            load_columns(2, w_in, KT, 2 * QK + RV, DV)
            load_rows(3, w_out, 0, DV)
            with sp.Fori(1, HEADS) as h:
                sp.wait_ge(lo_ready, 4 * TILES * h - 3 * TILES)
                load_head_qk(h)
                sp.wait_ge(lo_ready, 4 * TILES * h - 2 * TILES)
                load_columns(1, w_in, KT, h * DV + 2 * QK, DV)
                sp.wait_ge(lo_ready, 4 * TILES * h - TILES)
                load_columns(2, w_in, KT, h * DV + (2 * QK + RV), DV)
                sp.wait_ge(lo_ready, 4 * TILES * h)
                load_rows(3, w_out, h * DV, DV)

            def first_experts(l, tiles):
                sources = [(w_gate, 0, D), (w_up, 0, D), (w_down, 0, FF), (w_gate, 1, D), (w_up, 1, D), (w_down, 1, FF)]
                for s, (w, e, n) in enumerate(sources):
                    if s < 4:
                        sp.wait_ge(lo_ready, tiles[s])
                    elif s == 4:
                        sp.wait_ge(tile_used, NWT + tiles[4])
                    load_rows(s, w[l, e], 0, n)

            first_experts(0, [ret_tiles - n * TILES for n in (3, 2, 1, 0, 0)])

            for l in range(NL):
                sp.wait_ge(xn_ready, 4 * (2 * l + 2))
                sp.dma_start(xn_dram[l].rearrange("(i p q) c -> p i (q c)", i=NT, q=4), xn[:, :, :]) \
                    .then_inc(xn_stored[l], 16)
                gate_l = w_gate[l].rearrange("e d f -> (e d) f")
                up_l = w_up[l].rearrange("e d f -> (e d) f")
                down_l = w_down[l].rearrange("e f d -> (e f) d")
                sp.wait_ge(cum_ready[l], 1)
                if l == 1:
                    sp.dma_start(gfin[:, :], g_final.partition_broadcast(P)).then_inc(gfin_loaded, 16)
                with sp.Fori(1, NE // 2) as pair:
                    for odd in range(2):
                        s_gate, s_up, s_down = slots_of[odd]
                        upto = sp.value_load(cum[0:1, bass.ds(2 * pair + (odd - 1), 1)], min_val=1, max_val=NBLK - 1)
                        e = 2 * pair + odd
                        sp.wait_ge(gu_mm[l], upto)
                        load_rows(s_gate, gate_l, e * D, D)
                        load_rows(s_up, up_l, e * D, D)
                        sp.wait_ge(y_mm[l], upto)
                        load_rows(s_down, down_l, e * FF, FF)
                if l == 0:
                    total = sp.value_load(cum[0:1, NE:NE + 1], min_val=NE, max_val=NBLK - 1)
                    last = sp.value_load(cum[0:1, NE - 1:NE], min_val=1, max_val=NBLK - 1)
                    for j in range(4):
                        sp.wait_ge((gu_mm if j != 2 else y_mm)[l], last if j < 3 else total)
                        load_columns(j, w_pw1, KT, j * 2 * P, 2 * P)
                        load_columns(j, w_pw1, KT, j * 2 * P + D, 2 * P, at=2 * P)
                sp.wait_ge(rows_out[l], 1)
                for i in range(NT):
                    sp.dma_start(ytile[i], y_dram[l].rearrange("(t r) c -> t (r c)", r=8)[i * P:(i + 1) * P, :]) \
                        .then_inc(y_loaded[l][i], 16)
                if l == 0:
                    for n in range(2):
                        sp.wait_ge(lo_ready, ret_tiles + (n + 1) * TILES)
                        load_columns(n, w_pw2, KT, n * 512, 512)
                    split = ret_tiles + pw1_tiles
                    sp.wait_ge(lo_ready, split - TILES)
                    load_rows(2, w_down[1, 0], 0, FF)
                    sp.wait_ge(lo_ready, split)
                    load_rows(3, w_gate[1, 1], 0, D)
                    sp.wait_ge(lo_ready, split + TILES)
                    load_rows(0, w_gate[1, 0], 0, D)
                    sp.wait_ge(lo_ready, split + 2 * TILES)
                    load_rows(1, w_up[1, 0], 0, D)
                    sp.wait_ge(tile_used, NWT + split + 2 * TILES)
                    load_rows(4, w_up[1, 1], 0, D)
                    load_rows(5, w_down[1, 1], 0, FF)
            for i in range(NT):
                sp.wait_ge(xn_ready, 4 * 4 + i + 1)
                sp.dma_start(out[i * P:(i + 1) * P, :], xn[:, i, :]).then_inc(out_stored, 16)
            sp.wait_ge(out_stored, 16 * NT)

        @block.gpsimd
        def _(pool):
            def split_lo(n, place, s, at):
                pool.wait_ge(hi_ready, n + 1)
                nc.gpsimd.tensor_tensor(w_lo[:, place, :], ring[:, s, at:at + 512],
                                        w_hi[:, place, :].bitcast(F32), ALU.subtract).then_inc(lo_ready, 1)

            with pool.Fori(0, HEADS) as h:
                for s in range(4):
                    for k in range(TILES):
                        split_lo(4 * TILES * h + (s * TILES + k), k % NWT, s, tile_column(s == 3, k))

            gather_bound, scatter_bound = pool.to_reg(4 * S - 1), pool.to_reg(8 * S - 1)

            for l in range(NL):
                def gather(b):
                    pool.indirect_dma_start(
                        hg_in[:, b, :], None, xn_dram[l],
                        bass.IndirectOffsetOnAxis(ap=idx_g[:, b:b + 1].bitcast(U32), axis=0),
                        bounds_check=gather_bound, oob_is_err=False).then_inc(gathered[l][b], 16)

                def scatter(b):
                    pool.indirect_dma_start(
                        y_dram[l], bass.IndirectOffsetOnAxis(ap=idx_s[:, b:b + 1].bitcast(U32), axis=0),
                        y_out[:, b, :], None, bounds_check=scatter_bound, oob_is_err=False) \
                        .then_inc((scattered_lo if b < GRP // 2 else scattered_hi)[l], 16)

                if l == 1:
                    for n in range(pw1_tiles + 2 * TILES):
                        split_lo(ret_tiles + n, n % NWT, n // TILES % 4, tile_column(False, n % TILES))
                pool.wait_ge(idx_ready[l], 1)
                pool.wait_ge(xn_stored[l], 16)
                pool.tensor_copy(idx_g[:, :], idx[:, 1, 0:GRP]).then_inc(idx_copied[l], 1)
                pool.wait_ge(idx_copied[l], 1)
                for b in range(GRP):
                    gather(b)
                pool.sem_inc(y_free[l], GRP)
                for b in range(GRP // 2):
                    pool.wait_ge(gathered[l][b], 16)
                    pool.sem_inc(rows_in[l], 1)
                total = pool.value_load(cum[0:1, NE:NE + 1], min_val=NE, max_val=NBLK - GRP)
                steps = pool.value_load(cum[0:1, NE + 1:NE + 2], min_val=NE // GRP, max_val=NBLK // GRP - 1)
                for b in range(GRP):
                    pool.wait_ge(gathered[l][b], 16)
                with pool.Fori(0, steps) as g:
                    pool.tensor_copy(idx_g[:, :], idx[:, 1, bass.ds(GRP * g + GRP, GRP)]).then_inc(idx_copied[l], 1)
                    pool.tensor_copy(idx_s[:, :], idx[:, 0, bass.ds(GRP * g, GRP)]).then_inc(idx_copied[l], 1)
                    pool.wait_ge(idx_copied[l], 2 * g + 3)
                    for b in range(GRP):
                        ahead = (b + GRP // 2) % GRP
                        pool.wait_ge(gathered[l][ahead], 16 * g + (16 if ahead > b else 32))
                        pool.sem_inc(rows_in[l], 1)
                        pool.wait_ge(staged[l], GRP * g + (b + 1))
                        pool.nop(nofuse=True)
                        gather(b)
                        pool.wait_ge(y_ready[l], GRP * g + (b + 1))
                        pool.nop(nofuse=True)
                        scatter(b)
                        if b == GRP - 2:
                            pool.wait_ge(scattered_lo[l], 8 * GRP * g + 8 * GRP)
                            pool.sem_inc(y_free[l], GRP // 2)
                    pool.wait_ge(scattered_hi[l], 8 * GRP * g + 8 * GRP)
                    pool.sem_inc(y_free[l], GRP // 2)
                    for b in range(GRP):
                        pool.wait_ge(gathered[l][b], 16 * g + 32)
                pool.wait_ge(staged[l], total + 2)
                pool.sem_inc(rows_out[l], 1)

        @block.scalar
        def _(act):
            link = Link(act, act_link)

            def norm_roots(n, x_ready):
                for i in range(NT):
                    x_ready(i)
                    link.done(nc.scalar.activation(xn[:, i, :], x[:, i, :], ACT.Square, accum_out=ss[:, i:i + 1]))
                    nc.scalar.activation(rt[:, i:i + 1], ss[:, i:i + 1], ACT.Sqrt, bias=eps,
                                         scale=1.0 / D).then_inc(root_ready, 1)

            def split_hi(n, place, s, at):
                act.wait_ge(tile_used, n + 1)
                nc.scalar.copy(w_hi[:, place, :], ring[:, s, at:at + 512]).then_inc(hi_ready, 1)

            def norm_hi(n, m, gain):
                for k in range(KT):
                    act.wait_ge(hT_mm, KT * n + k + 1)
                    nc.scalar.activation(hT_hi[:, k, :], ps[:, k, :], ACT.Copy,
                                         scale=par[:, gain + k:gain + k + 1]).then_inc(hThi_ready, 1)

            def norm_turned(n, gain):
                for k in range(0, KT, 2):
                    act.wait_ge(hT_mm, KT * n + k + 1)
                    nc.scalar.activation(hT[:, k, :], ps[:, k, :], ACT.Copy,
                                         scale=par[:, gain + k:gain + k + 1]).then_inc(hT_even, 1)

            def expert_blocks(l):
                act.wait_ge(exp_arg[l], 1)
                nc.scalar.activation(small[:, 48:64], small[:, 48:64], ACT.Exp).then_inc(exp_ready[l], 1)
                act.wait_ge(exp_arg[l], 2)
                nc.scalar.activation(small[:, 48:52], small[:, 48:52], ACT.Exp).then_inc(exp_ready[l], 1)
                act.wait_ge(cum_ready[l], 1)
                total = act.value_load(cum[0:1, NE:NE + 1], min_val=NE, max_val=NBLK - 1)
                with act.Fori(0, total) as t:
                    act.wait_ge(gu_mm[l], t + 1)
                    nc.scalar.activation(sg_e[:, :], ps[:, 2, 0:P], ACT.Silu).then_inc(silu_ready[l], 1)
                    act.wait_ge(t2_mm[l], t + 1)
                    nc.scalar.copy(aT_e[:, :], ps[:, 3, 0:P]).then_inc(aT_ready[l], 1)
                    act.wait_ge(y_mm[l], t + 1)
                    act.wait_ge(y_free[l], t + 1)
                    nc.scalar.copy(area_c[:, bass.ds((t % GRP) * QW + 4096, QW)], ps[:, 4, 0:QW]) \
                        .then_inc(y_ready[l], 1)
                act.wait_ge(y_ready[l], total)
                act.sem_inc(y_ready[l], GRP)

            act.dma_start(const[:, :], const_in).then_inc(const_loaded, 16)
            act.dma_start(par[:, :], par_in).then_inc(par_loaded, 16)
            act.dma_start(area_b[:, 0:S].bitcast(I32), pos_in.partition_broadcast(P)).then_inc(pos_loaded, 16)
            act.dma_start(wr[:, :, :, :], w_router).then_inc(par_loaded, 16)
            act.dma_start(rows[0:1, 0:D], b_pw2).then_inc(par_loaded, 16)
            act.dma_start(rows[0:1, D:D + NL * (NG + NE)], b_router).then_inc(par_loaded, 16)
            act.wait_ge(pad_zero, 1)
            norm_roots(0, lambda i: act.wait_ge(x_loaded[i], 16))
            act.wait_ge(par_loaded, 64)
            norm_hi(0, 0, G_MIX)
            act.wait_ge(trig_arg, 1)
            nc.scalar.activation(trig[:, :, :], trig[:, :, :], ACT.Sin).then_inc(trig_ready, 1)
            with act.Fori(0, HEADS) as h:
                def split(s, first, last):
                    for k in range(first, last):
                        split_hi(4 * TILES * h + (s * TILES + k), k % NWT, s, tile_column(s == 3, k))

                act.wait_ge(slot_loaded[0], 32 * h + 32)
                split(0, 0, TILES)
                act.wait_ge(slot_loaded[1], 16 * h + 16)
                split(1, 0, TILES)
                act.wait_ge(slot_loaded[2], 16 * h + 16)
                split(2, 0, NWT)
                act.wait_ge(tile_used, 4 * TILES * h + (2 * TILES + NWT))
                for i in range(NT):
                    nc.scalar.copy(v[:, i, :], ps[:, 4 + i, :]).then_inc(v_ready, 1)
                split(2, NWT, TILES)
                act.wait_ge(slot_loaded[3], 16 * h + 16)
                split(3, 0, NWT)
                act.wait_ge(tile_used, 4 * TILES * h + (3 * TILES + NWT))
                for i in range(NT):
                    nc.scalar.activation(sg[:, i, :], ps[:, i, :], ACT.Silu).then_inc(sg_ready, 1)
                for i in range(NT):
                    act.wait_ge(pv_mm, 4 * h + (i + 1))
                    nc.scalar.activation(squares[:, i, :], ps[:, 4 + i, :], ACT.Square,
                                         accum_out=ss[:, i:i + 1]).then_inc(act_head, 1)
                    act.wait_ge(act_head, 4 * h + (i + 1))
                    nc.scalar.activation(rt[:, i:i + 1], ss[:, i:i + 1], ACT.Sqrt, bias=eps,
                                         scale=1.0 / DV).then_inc(oroot_ready, 1)
                for f in range(NT):
                    act.wait_ge(tr_mm, 4 * h + (f + 1))
                    nc.scalar.activation(oT_hi[:, f, :], ps[:, f, :], ACT.Copy,
                                         scale=par[:, bass.ds(4 * h + (G_HEAD + f), 1)]).then_inc(oT_ready, 1)
                split(3, NWT, TILES)
            norm_roots(1, lambda i: act.wait_ge(x_added, 8 * HEADS + 4 + i + 1 if i < 2 else 8 * HEADS + 8))
            norm_turned(1, G_FFN)
            expert_blocks(0)

            norm_roots(2, lambda i: act.wait_ge(combined, i + 1))
            norm_hi(2, 1, G_MIX + KT)

            def split_conv(first, last):
                for n in range(first, last):
                    if n % TILES == 0:
                        s = n // TILES % 4
                        act.wait_ge(slot_loaded[s], expert_base(0, s) + 16 * NE // 2 + (32 if n < pw1_tiles else 48))
                    split_hi(ret_tiles + n, n % NWT, n // TILES % 4, tile_column(False, n % TILES))

            split_conv(0, TILES)
            for j in range(4):
                split_conv((j + 1) * TILES, (j + 1) * TILES + NWT)
                act.wait_ge(tile_used, ret_tiles + (j + 1) * TILES + NWT)
                for c in (2 * j, 2 * j + 1):
                    if c >= 2:
                        act.wait_ge(u_ready, c - 1)
                    nc.scalar.activation(sig[:, c % 2, :], ps[:, 4 * (j % 2) + 2 + c % 2, :], ACT.Sigmoid,
                                         bias=par[:, B_PW1 + KT + c:B_PW1 + KT + c + 1]).then_inc(sig_ready, 1)
                if j < 3:
                    split_conv((j + 1) * TILES + NWT, (j + 2) * TILES)
            for n, (c, k) in enumerate((c, k) for c in PE_CHANNELS for k in range(WIDTH)):
                if n >= 8:
                    act.wait_ge(diag_used, n - 7)
                nc.scalar.activation(diag[:, n % 8, :], ident, ACT.Copy,
                                     scale=par[:, W_DW + c * WIDTH + k:W_DW + c * WIDTH + k + 1]) \
                    .then_inc(diag_ready, 1)
            for n, c in enumerate(PE_CHANNELS):
                act.wait_ge(diag_used, (n + 1) * WIDTH)
                nc.scalar.activation(z[:, c, :], ps[:, n, :], ACT.Identity,
                                     bias=par[:, B_DW + c:B_DW + c + 1]).then_inc(zpe_ready, 1)
            for i in range(NT):
                act.wait_ge(lnroot_ready, 2 * i + 1)
                nc.scalar.activation(rt[:, i:i + 1], mv[:, 2 * i + 1:2 * i + 2], ACT.Sqrt,
                                     bias=eps).then_inc(lnscale_ready, 1)
                act.wait_ge(lnroot_ready, 2 * i + 2)
                nc.scalar.activation(xn[:, i, :], ps[:, 2 * i:2 * i + 2, :].rearrange("p b s -> p (b s)"),
                                     ACT.Identity, bias=ss[:, i:i + 1], scale=rstd[:, i:i + 1]) \
                    .then_inc(zn_ready, 1)
            for k in range(KT):
                act.wait_ge(ztb_mm, k + 1)
                nc.scalar.activation(z[:, k, :], ps[:, k, :], ACT.Silu, bias=par[:, LN_B + k:LN_B + k + 1],
                                     scale=par[:, LN_G + k:LN_G + k + 1]).then_inc(zh_ready, 1)
                act.wait_ge(zh_ready, k + 1)
                nc.scalar.copy(hT_hi[:, k, :], z[:, k, :]).then_inc(hThi_ready, 1)
            split_conv(pw1_tiles + NWT, pw1_tiles + 2 * TILES)
            norm_roots(3, lambda i: act.wait_ge(x2_added, NT + i + 1))
            norm_turned(3, G_FFN + KT)
            expert_blocks(1)
            norm_roots(4, lambda i: act.wait_ge(combined, NT + i + 1))

        @block.tensor
        def _(pe):
            def turn_norm(n):
                for k in range(KT):
                    for i in range(NT):
                        if k == 0:
                            pe.wait_ge(xn_ready, 4 * n + i + 1)
                        last = nc.tensor.transpose(ps[:, k, i * P:(i + 1) * P], xn[:, i, k * P:(k + 1) * P], ident)
                    last.then_inc(hT_mm, 1)

            def wait_norm(l):
                pe.wait_ge(hT_even, 4 * (l + 1))
                pe.wait_ge(hT_odd, 4 * (l + 1))

            def three(at, lhs, rhs, start, stop):
                nc.tensor.matmul(at, lhs[0], rhs[0], start=start, stop=False)
                nc.tensor.matmul(at, lhs[0], rhs[1], start=False, stop=False)
                return nc.tensor.matmul(at, lhs[1], rhs[0], start=False, stop=stop)

            def product(number, bank, weights_stand, operand=None, last=True, tiles=range(TILES)):
                tokens = operand or (hT_hi, hT_lo)
                for k in tiles:
                    w = (w_hi[:, k % NWT, :], w_lo[:, k % NWT, :])
                    pe.wait_ge(lo_ready, number(k) + 1)
                    row = k % 4 if operand else k
                    for m in range(4):
                        cols = slice(m * P, (m + 1) * P)
                        start, stop = k == tiles[0], last and k == tiles[-1]
                        if weights_stand:
                            ins = three(ps[:, bank + m, :], [t[:, cols] for t in w], [t[:, row, :] for t in tokens],
                                        start, stop)
                        else:
                            ins = three(ps[:, bank + m, :], [t[:, row, cols] for t in tokens], w, start, stop)
                    ins.then_inc(tile_used, 1)

            def route(l):
                for i in range(NT):
                    at = ps[:, 0, i * 64:i * 64 + NG + NE]
                    for k in range(KT):
                        nc.tensor.matmul(at, hT[:, k, i * P:(i + 1) * P], wr[:, l, k, :], start=(k == 0), stop=False)
                    last = nc.tensor.matmul(at, const[0:1, C_ONE:C_ONE + P],
                                            rows[0:1, D + l * (NG + NE):D + (l + 1) * (NG + NE)],
                                            start=False, stop=True)
                last.then_inc(logit_mm[l], 1)
                pe.wait_ge(onehot_ready[l], 1)
                nc.tensor.matmul(ps[:, 5, 0:8 * NE], tri, onehot[:, :], start=True, stop=False)
                nc.tensor.matmul(ps[:, 5, 0:8 * NE], ones, before[:, 0:8 * NE], start=False, stop=True)
                nc.tensor.matmul(ps[:, 6, 0:NE], ones, before[:, 8 * NE:9 * NE], start=True, stop=True) \
                    .then_inc(rank_mm[l], 1)
                pe.wait_ge(spread_ready[l], 1)
                for j in range(8):
                    last = nc.tensor.matmul(ps[:, 7, 0:2 * NBLK], slot_hot[:, j, :], block_hot[:, j, :],
                                            start=(j == 0), stop=(j == 7))
                last.then_inc(idx_mm[l], 1)

            def turn_block(l, t):
                pe.wait_ge(staged[l], t + 1)
                for c in range(2):
                    last = nc.tensor.transpose(ps[:, 1, c * P:(c + 1) * P], hg[:, c * P:(c + 1) * P], ident)
                last.then_inc(t1_mm[l], 1)

            def one_block(l, t, pair, s_gate, s_up, s_down):
                gate_up = ring[:, s_gate:s_gate + 2, :].rearrange("p w (k f) -> p w k f", k=KT)
                down = ring[:, s_down, :].rearrange("p (k d) -> p k d", k=4)
                pe.wait_ge(hgT_ready[l], t + 1)
                for s in (s_gate, s_up):
                    pe.wait_ge(slot_loaded[s], 16 * pair + (expert_base(l, s) + 16))
                for k in range(KT):
                    for g in range(4):
                        last = nc.tensor.matmul(ps[32 * g:32 * g + 32, 2, 0:256], hgT[:, k, :],
                                                gate_up[:, :, k, g * P:(g + 1) * P],
                                                start=(k == 0), stop=(k == KT - 1), tile_position=(0, 32 * g))
                last.then_inc(gu_mm[l], 1)
                turn_block(l, t + 1)
                pe.wait_ge(act_ready[l], t + 1)
                nc.tensor.transpose(ps[:, 3, 0:P], a_e[:, :], ident).then_inc(t2_mm[l], 1)
                pe.wait_ge(aT_ready[l], t + 1)
                pe.wait_ge(slot_loaded[s_down], 16 * pair + (expert_base(l, s_down) + 16))
                for k in range(4):
                    for g in range(4):
                        last = nc.tensor.matmul(ps[32 * g:32 * g + 32, 4, 0:256], aT_e[:, k * BLK:(k + 1) * BLK],
                                                down[:, k, g * 256:(g + 1) * 256],
                                                start=(k == 0), stop=(k == 3), tile_position=(0, 32 * g))
                last.then_inc(y_mm[l], 1)

            def experts(l):
                turn_block(l, 0)
                with pe.Fori(0, NE // 2) as pair:
                    for odd in range(2):
                        slots = slots_of[odd]
                        first = pe.value_load(cum[0:1, bass.ds(2 * pair + odd, 1)], min_val=0, max_val=NBLK - 2)
                        after = pe.value_load(cum[0:1, bass.ds(2 * pair + (odd + 1), 1)], min_val=1, max_val=NBLK - 1)
                        with pe.Fori(first, after) as t:
                            one_block(l, t, pair, *slots)

            pe.sem_inc(tile_used, NWT)
            pe.wait_ge(const_loaded, 16)
            turn_norm(0)
            pe.wait_ge(hThi_ready, KT)
            pe.wait_ge(hTlo_ready, KT)
            with pe.Fori(0, HEADS) as h:
                def tile(s):
                    return lambda k: 4 * TILES * h + (s * TILES + k)

                pe.wait_ge(x_added, 8 * h + 4)
                product(tile(0), 0, True)
                pe.wait_ge(x_added, 8 * h + 8)
                product(tile(1), 4, False)
                pe.wait_ge(rot_ready, 4 * h + 4)
                for j in range(NT):
                    pe.wait_ge(v_ready, 4 * h + (j + 1))
                    for d in range(2):
                        last = nc.tensor.matmul(ps[:, 4 + j, 0:S - j * P], kT[:, d, j * P:(j + 1) * P],
                                                qT[:, d, j * P:S], start=(d == 0), stop=(d == 1))
                    last.then_inc(sc_mm, 1)
                product(tile(2), 0, False)
                pe.wait_ge(sT_ready, 4 * h + 4)
                for i in range(NT):
                    for j in range(i + 1):
                        last = nc.tensor.matmul(ps[:, 4 + i, :], sT[:, j, i * P:(i + 1) * P], v[:, j, :],
                                                start=(j == 0), stop=(j == i))
                    last.then_inc(pv_mm, 1)
                pe.wait_ge(on_ready, 4 * h + 4)
                for f in range(NT):
                    for i in range(NT):
                        last = nc.tensor.transpose(ps[:, f, i * P:(i + 1) * P], sg[:, i, f * P:(f + 1) * P], ident)
                    last.then_inc(tr_mm, 1)
                pe.wait_ge(oT_ready, 4 * h + 4)
                pe.wait_ge(oTlo_ready, 4 * h + 4)
                for n in range(2):
                    product(tile(3), 4 * n, False, operand=(oT_hi, oT_lo), tiles=range(4 * n, 4 * n + 4))
            turn_norm(1)
            wait_norm(0)
            route(0)
            experts(0)

            turn_norm(2)
            pe.wait_ge(hThi_ready, 2 * KT)
            pe.wait_ge(hTlo_ready, 2 * KT)
            for j in range(4):
                if j >= 2:
                    pe.wait_ge(u_ready, 2 * j - 2)
                product(lambda k: ret_tiles + j * TILES + k, 4 * (j % 2), True)
            n = 0
            pe.wait_ge(u_ready, 6)
            for m, c in enumerate(PE_CHANNELS):
                for k in range(WIDTH):
                    pe.wait_ge(diag_ready, n + 1)
                    nc.tensor.matmul(ps[:, m, :], diag[:, n % 8, :], uT[:, c, k:k + S],
                                     start=(k == 0), stop=(k == WIDTH - 1)).then_inc(diag_used, 1)
                    n += 1
            pe.wait_ge(u_ready, KT)
            pe.wait_ge(zpe_ready, 2)
            for c in PE_CHANNELS + DVE_CHANNELS:
                if c in DVE_CHANNELS:
                    pe.wait_ge(z_ready, DVE_CHANNELS.index(c) + 1)
                for i in range(NT):
                    last = nc.tensor.transpose(ps[:, 2 * i + c // 4, (c % 4) * P:(c % 4 + 1) * P],
                                               z[:, c, i * P:(i + 1) * P], ident)
            last.then_inc(zt_mm, 1)
            pe.wait_ge(zn_ready, NT)
            for k in range(KT):
                for i in range(NT):
                    last = nc.tensor.transpose(ps[:, k, i * P:(i + 1) * P], xn[:, i, k * P:(k + 1) * P], ident)
                last.then_inc(ztb_mm, 1)
            pe.wait_ge(hThi_ready, 3 * KT)
            pe.wait_ge(hTlo_ready, 3 * KT)
            for n in range(2):
                product(lambda k: ret_tiles + pw1_tiles + n * TILES + k, 4 * n, False, last=False)
                for i in range(NT):
                    nc.tensor.matmul(ps[:, 4 * n + i, :], const[0:1, C_ONE:C_ONE + P], rows[0:1, n * 512:(n + 1) * 512],
                                     start=False, stop=True).then_inc(pw2_mm, 1)
            turn_norm(3)
            wait_norm(1)
            route(1)
            experts(1)

        @block.vector
        def _(dve):
            link = Link(dve, dve_link)
            V = nc.vector

            def scale_norm(n):
                for i in range(NT):
                    dve.wait_ge(root_ready, 4 * n + i + 1)
                    link.done(V.reciprocal(rstd[:, i:i + 1], rt[:, i:i + 1]))
                    if n < 4:
                        V.tensor_scalar(xn[:, i, :], x[:, i, :], rstd[:, i:i + 1], None, ALU.mult) \
                            .then_inc(xn_ready, 1)
                    else:
                        V.scalar_tensor_tensor(out=xn[:, i, :], in0=x[:, i, :], scalar=rstd[:, i:i + 1],
                                               in1=gfin[:, :], op0=ALU.mult, op1=ALU.mult).then_inc(xn_ready, 1)

            def turned_norm(n, gain):
                for k in range(1, KT, 2):
                    dve.wait_ge(hT_mm, KT * n + k + 1)
                    V.tensor_scalar(hT[:, k, :], ps[:, k, :], par[:, gain + k:gain + k + 1], None, ALU.mult) \
                        .then_inc(hT_odd, 1)

            def norm_lo(n, m, gain):
                for k in range(KT):
                    dve.wait_ge(hThi_ready, KT * m + k + 1)
                    V.scalar_tensor_tensor(out=hT_lo[:, k, :], in0=ps[:, k, :], scalar=par[:, gain + k:gain + k + 1],
                                           in1=hT_hi[:, k, :].bitcast(F32), op0=ALU.mult, op1=ALU.subtract) \
                        .then_inc(hTlo_ready, 1)

            def first_max(l, scores, best, rev, n, oh):
                shape = [P, NT, n]
                link.done(V.tensor_tensor(eq[:, :, 0:n], scores, best.unsqueeze(2).to_broadcast(shape), ALU.is_equal))
                link.done(V.tensor_tensor(eq[:, :, 0:n], eq[:, :, 0:n], rev.unsqueeze(1).to_broadcast(shape), ALU.mult))
                link.done(V.tensor_reduce(pick[:, :], eq[:, :, 0:n], AX, ALU.max))
                link.done(V.tensor_tensor(oh, eq[:, :, 0:n], pick[:, :].unsqueeze(2).to_broadcast(shape), ALU.is_equal))

            def route(l):
                dve.wait_ge(logit_mm[l], 1)
                link.done(V.tensor_copy(logits[:, :, :], ps[:, 0, 0:256].rearrange("p (i e) -> p i e", i=NT)
                                        [:, :, 0:NG + NE]))
                lg = logits[:, :, 0:NG]
                link.done(V.tensor_reduce(best[:, :], lg, AX, ALU.max))
                V.tensor_tensor(small[:, 48:64].rearrange("p (i g) -> p i g", i=NT), lg,
                                best[:, :].unsqueeze(2).to_broadcast([P, NT, NG]), ALU.subtract) \
                    .then_inc(exp_arg[l], 1)
                first_max(l, lg, best[:, :], const[:, C_REV4:C_REV4 + NG], NG, group_hot[:, :, :])
                dve.wait_ge(exp_ready[l], 1)
                link.done(V.tensor_reduce(gate[:, :], small[:, 48:64].rearrange("p (i g) -> p i g", i=NT), AX, ALU.add))
                link.done(V.reciprocal(gate[:, :], gate[:, :]))
                link.done(V.tensor_scalar(group_hot[:, :, :], group_hot[:, :, :], -1.0, FAR, ALU.add, ALU.mult))
                for i in range(NT):
                    link.sent(V.tensor_tensor(
                        le[:, i, :].rearrange("p (g e) -> p g e", g=NG),
                        logits[:, i, NG:NG + NE].rearrange("p (g e) -> p g e", g=NG),
                        group_hot[:, i, :].unsqueeze(2).to_broadcast([P, NG, NPG]), ALU.add))
                link.wait()
                rev = const[:, C_REV32:C_REV32 + NE]
                oh = onehot[:, :].rearrange("p (j e) -> p j e", j=8)
                link.done(V.tensor_reduce(best[:, :], le[:, :, :], AX, ALU.max))
                first_max(l, le[:, :, :], best[:, :], rev, NE, oh[:, 0:NT, :])
                link.done(V.scalar_tensor_tensor(out=le[:, :, :], in0=oh[:, 0:NT, :], scalar=-3.0 * FAR,
                                                 in1=le[:, :, :], op0=ALU.mult, op1=ALU.add))
                link.done(V.tensor_reduce(second[:, :], le[:, :, :], AX, ALU.max))
                V.tensor_tensor(small[:, 48:52], second[:, :], best[:, :], ALU.subtract).then_inc(exp_arg[l], 1)
                first_max(l, le[:, :, :], second[:, :], rev, NE, oh[:, NT:2 * NT, :])
                link.done(V.memset(before[:, 0:NE], 0.0))
                for j in range(8):
                    ins = V.tensor_tensor(before[:, (j + 1) * NE:(j + 2) * NE], before[:, j * NE:(j + 1) * NE],
                                          onehot[:, j * NE:(j + 1) * NE], ALU.add)
                    if j < 7:
                        link.done(ins)
                ins.then_inc(onehot_ready[l], 1)
                dve.wait_ge(exp_ready[l], 2)
                link.done(V.tensor_scalar(second[:, :], small[:, 48:52], 1.0, None, ALU.add))
                link.done(V.reciprocal(second[:, :], second[:, :]))
                link.done(V.tensor_tensor(wts[:, 0, :], second[:, :], gate[:, :], ALU.mult))
                link.done(V.tensor_tensor(wts[:, 1, :], wts[:, 0, :], small[:, 48:52], ALU.mult))
                dve.wait_ge(rank_mm[l], 1)
                link.done(V.tensor_scalar(count[:, :], ps[:, 6, 0:NE], BLK - 1.0, None, ALU.add))
                link.done(V.tensor_single_scalar(count[:, :], count[:, :], 5, ALU.arith_shift_right))
                link.done(V.tensor_scalar(blocks[:, :], count[:, :], 1.0, None, ALU.max))
                link.done(V.tensor_tensor_scan(upto[:, :], blocks[:, :], blocks[:, :], 0.0, ALU.add, ALU.bypass))
                link.sent(V.tensor_copy(cum[:, 1:NE + 1], upto[:, :]))
                link.done(V.tensor_scalar(count[:, 0:1], upto[:, NE - 1:NE], GRP - 1.0, None, ALU.add))
                V.tensor_single_scalar(cum[:, NE + 1:NE + 2], count[:, 0:1], 3, ALU.arith_shift_right) \
                    .then_inc(cum_ready[l], 1)
                link.done(V.tensor_tensor(upto[:, :], upto[:, :], blocks[:, :], ALU.subtract))
                rank3 = ps[:, 5, 0:8 * NE].rearrange("p (j e) -> p j e", j=8)
                link.done(V.tensor_tensor(work[:, :, :], rank3, oh, ALU.mult))
                link.done(V.tensor_reduce(rank[:, :], work[:, :, :], AX, ALU.add))
                link.done(V.tensor_tensor(work[:, :, :], oh, upto[:, :].unsqueeze(1).to_broadcast([P, 8, NE]), ALU.mult))
                link.done(V.tensor_reduce(base[:, :], work[:, :, :], AX, ALU.add))
                link.done(V.tensor_copy(ranki[:, :], rank[:, :]))
                link.done(V.tensor_single_scalar(blki[:, :], ranki[:, :], 5, ALU.arith_shift_right))
                link.done(V.tensor_single_scalar(ranki[:, :], ranki[:, :], BLK - 1, ALU.bitwise_and))
                link.done(V.tensor_copy(rank[:, :], ranki[:, :]))
                link.done(V.tensor_tensor(base[:, :], base[:, :], blki[:, :], ALU.add))
                link.sent(V.tensor_tensor(slot_hot[:, :, :],
                                          const[:, C_MOD:C_MOD + P].unsqueeze(1).to_broadcast([P, 8, P]),
                                          rank[:, :].unsqueeze(2).to_broadcast([P, 8, P]), ALU.is_equal))
                link.done(V.tensor_tensor(block_hot[:, :, 0:NBLK],
                                          const[:, C_IOTA:C_IOTA + NBLK].unsqueeze(1).to_broadcast([P, 8, NBLK]),
                                          base[:, :].unsqueeze(2).to_broadcast([P, 8, NBLK]), ALU.is_equal))
                link.done(V.tensor_tensor(block_hot[:, :, NBLK:2 * NBLK], block_hot[:, :, 0:NBLK],
                                          const[:, C_TOK:C_TOK + 8].unsqueeze(2).to_broadcast([P, 8, NBLK]), ALU.mult))
                V.tensor_tensor(block_hot[:, :, 0:NBLK], block_hot[:, :, 0:NBLK],
                                const[:, C_A:C_A + 8].unsqueeze(2).to_broadcast([P, 8, NBLK]), ALU.mult) \
                    .then_inc(spread_ready[l], 1)
                dve.wait_ge(idx_mm[l], 1)
                dve.wait_ge(spread_ready[l], 1)
                table = before[:, 0:2 * NBLK]
                link.done(V.tensor_scalar(table, ps[:, 7, 0:2 * NBLK], 0.0, BIG, ALU.is_equal, ALU.mult))
                link.done(V.tensor_tensor(table, table, ps[:, 7, 0:2 * NBLK], ALU.add))
                V.tensor_scalar(idx[:, :, :], table.rearrange("p (a b) -> p a b", a=2), 4.0, const[:, C_QOFF:C_QOFF + 1],
                                ALU.mult, ALU.add).then_inc(idx_ready[l], 1)

            def turned_block(l, t, gain):
                for c in range(2):
                    ins = V.tensor_tensor(
                        hgT[:, :, :].rearrange("p (q c) s -> p c q s", c=2)[:, c],
                        ps[:, 1, c * P:(c + 1) * P].rearrange("p (q s) -> p q s", q=4),
                        par[:, gain:gain + KT].rearrange("p (q c) -> p c q", c=2)[:, c].unsqueeze(2)
                        .to_broadcast([P, 4, BLK]), ALU.mult)
                ins.then_inc(hgT_ready[l], 1)

            def stage(l, t):
                dve.wait_ge(rows_in[l], t + 1)
                V.tensor_copy(hg[:, :], area_a[:, bass.ds((t % GRP) * QW, QW)]).then_inc(staged[l], 1)

            def expert_blocks(l):
                gain = G_FFN + KT * l
                total = dve.value_load(cum[0:1, NE:NE + 1], min_val=NE, max_val=NBLK - 1)
                stage(l, 0)
                dve.wait_ge(t1_mm[l], 1)
                turned_block(l, 0, gain)
                stage(l, 1)
                with dve.Fori(0, total) as t:
                    dve.wait_ge(silu_ready[l], t + 1)
                    V.tensor_tensor(a_e[:, :], sg_e[:, :], ps[:, 2, P:2 * P], ALU.mult).then_inc(act_ready[l], 1)
                    dve.wait_ge(t1_mm[l], t + 2)
                    dve.wait_ge(gu_mm[l], t + 1)
                    turned_block(l, t + 1, gain)
                    stage(l, t + 2)
                dve.wait_ge(staged[l], total + 2)
                dve.sem_inc(staged[l], GRP)

            def combine(l):
                for i in range(NT):
                    dve.wait_ge(y_loaded[l][i], 16)
                    for k in range(2):
                        ins = V.scalar_tensor_tensor(out=x[:, i, :], in0=ytile[i][:, k * D:(k + 1) * D],
                                                     scalar=wts[:, k, i:i + 1], in1=x[:, i, :],
                                                     op0=ALU.mult, op1=ALU.add)
                        if k == 0:
                            link.done(ins)
                    ins.then_inc(combined, 1)

            V.memset(small[:, 0:4], EPS).then_inc(pad_zero, 1)
            link.done(V.memset(cum[:, 0:1], 0))
            dve.wait_ge(const_loaded, 16)
            dve.wait_ge(pos_loaded, 16)
            ang, turns, low, wrap = (tmp[:, n, :] for n in range(4))
            sin, cos = trig[:, 0, :], trig[:, 1, :]
            link.done(V.tensor_copy(ang, area_b[:, 0:S].bitcast(I32)))
            link.done(V.tensor_scalar(ang, ang, const[:, C_INV:C_INV + 1], None, ALU.mult))
            link.done(V.tensor_scalar(turns, ang, 1.0 / TWO_PI, ROUND, ALU.mult, ALU.add))
            link.done(V.tensor_scalar(turns, turns, ROUND, None, ALU.subtract))
            for part in TURN:
                link.done(V.scalar_tensor_tensor(out=ang, in0=turns, scalar=-part, in1=ang, op0=ALU.mult, op1=ALU.add))
            link.done(V.tensor_scalar(low, ang, TWO_PI / 4, None, ALU.add))
            link.done(V.tensor_scalar(wrap, low, PI, -TWO_PI, ALU.is_gt, ALU.mult))
            link.done(V.tensor_tensor(low, low, wrap, ALU.add))
            link.done(V.tensor_scalar(sin, ang, PI, -PI, ALU.min, ALU.max))
            V.tensor_scalar(cos, low, PI, -PI, ALU.min, ALU.max).then_inc(trig_arg, 1)
            scale_norm(0)
            dve.wait_ge(par_loaded, 64)
            norm_lo(0, 0, G_MIX)
            V.sem_inc(x_added, 8)
            dve.wait_ge(trig_ready, 1)
            dve.wait_ge(decay_loaded, 16)
            with dve.Fori(0, HEADS) as h:
                for n, dst in enumerate((qT, kT)):
                    lo, hi = ps[:, 2 * n, :], ps[:, 2 * n + 1, :]
                    if n == 0:
                        dve.wait_ge(tile_used, 4 * TILES * h + (TILES + NWT))
                    if n == 1:
                        dve.wait_ge(rot_ready, 4 * h + 2)
                    V.tensor_tensor(tmp[:, 0, :], lo, cos, ALU.mult)
                    V.tensor_tensor(tmp[:, 1, :], hi, sin, ALU.mult)
                    V.tensor_tensor(tmp[:, 2, :], lo, sin, ALU.mult)
                    V.tensor_tensor(tmp[:, 3, :], hi, cos, ALU.mult).then_inc(dve_head, 1)
                    dve.wait_ge(dve_head, 2 * h + (n + 1))
                    V.tensor_tensor(dst[:, 0, :], tmp[:, 0, :], tmp[:, 1, :], ALU.subtract).then_inc(rot_ready, 1)
                    V.tensor_tensor(dst[:, 1, :], tmp[:, 2, :], tmp[:, 3, :], ALU.add).then_inc(rot_ready, 1)
                for j in range(NT):
                    dve.wait_ge(sc_mm, 4 * h + (j + 1))
                    V.tensor_tensor(sT[:, j, j * P:S], ps[:, 4 + j, 0:S - j * P],
                                    decay[:, bass.ds(h, 1), 0:S - j * P].rearrange("p a s -> p (a s)"),
                                    ALU.mult).then_inc(sT_ready, 1)
                for i in range(NT):
                    dve.wait_ge(oroot_ready, 4 * h + (i + 1))
                    V.reciprocal(rstd[:, i:i + 1], rt[:, i:i + 1]).then_inc(dve_norm, 1)
                    dve.wait_ge(dve_norm, 4 * h + (i + 1))
                    dve.wait_ge(sg_ready, 4 * h + (i + 1))
                    V.scalar_tensor_tensor(out=sg[:, i, :], in0=ps[:, 4 + i, :], scalar=rstd[:, i:i + 1],
                                           in1=sg[:, i, :], op0=ALU.mult, op1=ALU.mult).then_inc(on_ready, 1)
                for f in range(NT):
                    dve.wait_ge(oT_ready, 4 * h + (f + 1))
                    V.scalar_tensor_tensor(out=oT_lo[:, f, :], in0=ps[:, f, :],
                                           scalar=par[:, bass.ds(4 * h + (G_HEAD + f), 1)],
                                           in1=oT_hi[:, f, :].bitcast(F32), op0=ALU.mult, op1=ALU.subtract) \
                        .then_inc(oTlo_ready, 1)
                for m in range(8):
                    i, n = m % 4, m // 4
                    if i == 0:
                        dve.wait_ge(tile_used, 4 * TILES * h + (3 * TILES + 4 * (n + 1) + NWT))
                    V.tensor_tensor(x[:, i, n * 512:(n + 1) * 512], x[:, i, n * 512:(n + 1) * 512], ps[:, m, :],
                                    ALU.add).then_inc(x_added, 1)
            dve.wait_ge(x_added, 8 * HEADS + 8)
            scale_norm(1)
            turned_norm(1, G_FFN)
            route(0)
            expert_blocks(0)
            combine(0)

            scale_norm(2)
            norm_lo(2, 1, G_MIX + KT)
            link.done(V.memset(uT[:, :, 0:PAD], 0.0))

            def glu(j):
                for c in (2 * j, 2 * j + 1):
                    dve.wait_ge(sig_ready, c + 1)
                    V.scalar_tensor_tensor(out=uT[:, c, PAD:PAD + S], in0=ps[:, 4 * (j % 2) + c % 2, :],
                                           scalar=par[:, B_PW1 + c:B_PW1 + c + 1], in1=sig[:, c % 2, :],
                                           op0=ALU.add, op1=ALU.mult).then_inc(u_ready, 1)

            for pair, channels in enumerate(zip(DVE_CHANNELS[::2], DVE_CHANNELS[1::2])):
                for j in ((0,), (1, 2), (3,))[pair]:
                    glu(j)
                dve.wait_ge(u_ready, (2, 6, 8)[pair])
                for k in range(WIDTH):
                    for c in channels:
                        tap = par[:, W_DW + c * WIDTH + k:W_DW + c * WIDTH + k + 1]
                        if k == 0:
                            ins = V.tensor_scalar(z[:, c, :], uT[:, c, 0:S], tap, par[:, B_DW + c:B_DW + c + 1],
                                                  ALU.mult, ALU.add)
                        else:
                            dve.wait_ge(dve_conv, 2 * (pair * (WIDTH - 1) + k - 1) + c % 2 + 1)
                            ins = V.scalar_tensor_tensor(out=z[:, c, :], in0=uT[:, c, k:k + S], scalar=tap,
                                                         in1=z[:, c, :], op0=ALU.mult, op1=ALU.add)
                        ins.then_inc(dve_conv if k < WIDTH - 1 else z_ready, 1)
            dve.wait_ge(zt_mm, 1)
            for i in range(NT):
                st = stats[:, 12 * (i % 2):12 * (i % 2) + 12]
                for b in range(2):
                    link.sent(V.bn_stats(st[:, 6 * b:6 * b + 6], ps[:, 2 * i + b, :]))
                link.wait()
                V.bn_aggr(mv[:, 2 * i:2 * i + 2], st).then_inc(lnroot_ready, 1)
                dve.wait_ge(lnscale_ready, i + 1)
                link.done(V.reciprocal(rstd[:, i:i + 1], rt[:, i:i + 1]))
                V.scalar_tensor_tensor(out=ss[:, i:i + 1], in0=mv[:, 2 * i:2 * i + 1], scalar=-1.0,
                                       in1=rstd[:, i:i + 1], op0=ALU.mult, op1=ALU.mult).then_inc(lnroot_ready, 1)
            for k in range(KT):
                dve.wait_ge(hThi_ready, 2 * KT + k + 1)
                V.tensor_tensor(hT_lo[:, k, :], z[:, k, :], hT_hi[:, k, :].bitcast(F32), ALU.subtract) \
                    .then_inc(hTlo_ready, 1)
            for n in range(2):
                for i in range(NT):
                    dve.wait_ge(pw2_mm, 4 * n + i + 1)
                    V.tensor_tensor(x[:, i, n * 512:(n + 1) * 512], x[:, i, n * 512:(n + 1) * 512],
                                    ps[:, 4 * n + i, :], ALU.add).then_inc(x2_added, 1)
            scale_norm(3)
            turned_norm(3, G_FFN + KT)
            route(1)
            expert_blocks(1)
            combine(1)
            dve.wait_ge(gfin_loaded, 16)
            scale_norm(4)


_NAMES = ("x_in", "pos_in", "const_in", "decay_in", "par_in", "w_in", "w_out", "w_pw1", "w_pw2", "b_pw2",
          "w_router", "b_router", "w_gate", "w_up", "w_down", "g_final")


def shape_constants():
    c = np.zeros((P, NCONST), np.float32)
    p = np.arange(P)
    c[:, C_ID:C_ID + P] = np.eye(P)
    c[:, C_TRI:C_TRI + P] = p[:, None] < p[None, :]
    c[:, C_ONE:C_ONE + P] = 1.0
    c[:, C_IOTA:C_IOTA + NBLK] = np.arange(NBLK)
    c[:, C_MOD:C_MOD + P] = p % BLK
    c[:, C_INV] = np.float32(10000.0) ** (-np.arange(P, dtype=np.float32) / np.float32(P))
    c[:, C_QOFF] = p // BLK - 4
    c[:, C_REV4:C_REV4 + NG] = NG - np.arange(NG)
    c[:, C_REV32:C_REV32 + NE] = NE - np.arange(NE)
    for j in range(8):
        tok = (j % NT) * P + p
        c[:, C_A + j] = 2 * tok + j // NT + 1
        c[:, C_TOK + j] = tok + 1
    gap = np.arange(S)[None, :] - p[:, None]
    decay = np.zeros((HEADS, P, S), np.float64)
    for h in range(HEADS):
        decay[h] = np.where(gap >= 0, (1.0 - 2.0 ** (-5.0 - h)) ** np.maximum(gap, 0), 0.0) * DK ** -0.5
    return c, decay.astype(np.float32)


def kernel(**inputs):
    import concourse.bacc as bacc
    from concourse.bass_utils import run_bass_kernel_spmd

    a = {k: np.asarray(v) for k, v in inputs.items()}
    const, decay = shape_constants()

    def columns(w):
        return w.reshape(-1, P).T

    taps = a["conv_w_dw"][0].reshape(WIDTH, KT, P).transpose(2, 1, 0).reshape(P, KT * WIDTH)
    par = np.concatenate([columns(a["norm_mix_g"]), columns(a["norm_ffn_g"]), columns(a["ret_head_g"]),
                          columns(a["conv_b_pw1"]), columns(a["conv_b_dw"]), columns(a["conv_ln_g"]),
                          columns(a["conv_ln_b"]), taps], axis=1)
    router = np.concatenate([a["moe_w_rg"], a["moe_w_re"]], axis=2).reshape(NL, KT, P, NG + NE)
    arrays = {
        "x_in": a["x"][0], "pos_in": a["positions"], "const_in": const, "decay_in": decay, "par_in": par,
        "w_in": a["ret_w_in"][0], "w_out": a["ret_w_out"][0], "w_pw1": a["conv_w_pw1"][0],
        "w_pw2": a["conv_w_pw2"][0], "b_pw2": a["conv_b_pw2"], "w_router": router.transpose(2, 0, 1, 3),
        "b_router": np.concatenate([a["moe_b_rg"], a["moe_b_re"]], axis=1).reshape(1, NL * (NG + NE)),
        "w_gate": a["moe_w_gate"], "w_up": a["moe_w_up"], "w_down": a["moe_w_down"],
        "g_final": a["final_norm_g"].reshape(1, D),
    }
    arrays = {k: np.ascontiguousarray(v) for k, v in arrays.items()}
    nc = bacc.Bacc("TRN2", target_bir_lowering=False, num_devices=1)
    aps = [nc.dram_tensor(n, arrays[n].shape, mybir.dt.from_np(arrays[n].dtype), kind="ExternalInput").ap()
           for n in _NAMES]
    out = nc.dram_tensor("out", (S, D), F32, kind="ExternalOutput").ap()
    program(nc, *aps, out)
    r = run_bass_kernel_spmd(nc, [arrays], core_ids=[0])
    return np.asarray(r.results[0]["out"]).reshape(1, S, D)
```

```python
from contextlib import ExitStack

import numpy as np
import concourse.bass as bass
from concourse import mybir

ALU = mybir.AluOpType
ACT = mybir.ActivationFunctionType
F32 = mybir.dt.float32
F32R = mybir.dt.float32r
I32 = mybir.dt.int32
U32 = mybir.dt.uint32
AX = mybir.AxisListType.X

P = 128
S = 512
D = 1024
NT = S // P
KT = D // P
HEADS, DK, DV = 4, 256, 512
QK, RV = HEADS * DK, HEADS * DV
WIDTH = 31
PAD = WIDTH - 1
NG, NPG = 4, 8
NE = NG * NPG
FF = 512
NL = 2
EPS = 1e-6
BLK = 32
QW = D // 4
GRP = 8
NBLK = 72
BIG = 1.0e6
FAR = 1.0e30
SLOT = 4096
NSLOT = 6
NWT = 4
TILES = 8

C_ID, C_TRI, C_ONE, C_IOTA, C_MOD = 0, 128, 256, 384, 456
C_INV, C_QOFF, C_REV4, C_REV32, C_A = 584, 585, 586, 590, 622
NCONST = 630
G_MIX, G_FFN, G_HEAD, B_PW1, B_DW, LN_G, LN_B, W_DW = 0, 16, 32, 48, 64, 72, 80, 88
NPAR = W_DW + KT * WIDTH

SPARE = (NE - 3, NE - 2, NE - 1)

PE_CHANNELS = (2, 3)
DVE_CHANNELS = (0, 1, 4, 5, 6, 7)
SHARED, SHARED_TAPS = 7, 12

TWO_PI = 6.283185307179586
PI = 3.1415925
ROUND = 12582912.0
TURN = (6.28125, 0.0019350051879882812, 3.0199159819567e-07)


class Link:

    def __init__(self, eng, sem):
        self.eng, self.sem, self.n = eng, sem, 0

    def sent(self, ins):
        ins.then_inc(self.sem, 1)
        self.n = self.n + 1

    def wait(self):
        self.eng.wait_ge(self.sem, self.n)

    def done(self, ins):
        self.sent(ins)
        self.wait()


def program(nc, x_in, pos_in, const_in, decay_in, par_in, w_in, w_out, w_pw1, w_pw2, b_pw2,
            w_router, b_router, w_gate, w_up, w_down, g_final, out):
    with ExitStack() as ctx:
        def sb(name, shape, dt=F32):
            return ctx.enter_context(nc.sbuf_tensor(name, shape, dt))

        def sem(name):
            return ctx.enter_context(nc.semaphore(name))

        def sems(name, n):
            return [sem(f"{name}{i}") for i in range(n)]

        def next_tensor():
            return -(-nc.sbuf_base // 32) * 32

        ps = ctx.enter_context(nc.psum_tensor("ps", [P, 8, 512], F32))

        ring_at = next_tensor()
        ring = sb("ring", [P, NSLOT, SLOT])
        x = sb("x", [P, NT, D])
        hT_at = next_tensor()
        hT = sb("hT", [P, KT, S])
        area_a_at = next_tensor()
        area_a = sb("area_a", [P, 4096])
        area_b_at = next_tensor()
        area_b = sb("area_b", [P, KT * (S + PAD)])
        area_c_at = next_tensor()
        area_c = sb("area_c", [P, 6144])
        trig = sb("trig", [P, 2, S])
        const = sb("const", [P, NCONST])
        par = sb("par", [P, NPAR])
        wr = sb("wr", [P, NL, KT, NG + NE])
        bias_2 = sb("bias_2", [1, D])
        bias_r = sb("bias_r", [P, NL, NG + NE])
        small = sb("small", [P, 64])
        counting = sb("counting", [P, 2, P], F32R)
        cum = sb("cum", [P, NE + 2], I32)
        idx = sb("idx", [P, NBLK], I32)
        idx_s = sb("idx_s", [P, GRP], I32)
        wts = sb("wts", [P, 2, NT])
        pos = sb("pos", [P, 2 * NT])
        both_hot = sb("both_hot", [P, 2 * NT, BLK])
        block_rows = sb("block_rows", [P, NT, BLK])
        hg = sb("hg", [P, QW])
        hgT = sb("hgT", [P, KT, BLK])
        sg_e = sb("sg_e", [P, P])
        a_e = sb("a_e", [P, P])
        aT_e = sb("aT_e", [P, P])

        def over(name, shape, under, words):
            return nc.alloc_sbuf_tensor_at(name, shape, F32R, offset=under + 4 * words)

        hT_hi = over("hT_hi", [P, KT, S], hT_at, 0)
        w_hi = over("w_hi", [P, NWT, 512], ring_at, 4 * SLOT)
        w_lo = over("w_lo", [P, NWT, 512], ring_at, 4 * SLOT + NWT * 512)
        hT_lo = over("hT_lo", [P, KT, S], ring_at, 5 * SLOT)
        oT_hi = over("oT_hi", [P, NT, S], area_a_at, 2048)
        oT_lo = over("oT_lo", [P, NT, S], area_c_at, 2048)

        onehot_r = over("onehot_r", [P, (NT * 2 + 1) * NE], area_b_at, 400)
        slot_hot_r = over("slot_hot_r", [P, 8, P], area_c_at, 0)
        block_hot_r = over("block_hot_r", [P, 8, NBLK], area_c_at, 8 * P)

        ident = const[:, C_ID:C_ID + P]
        ones = const[:, C_ONE:C_ONE + P]
        eps = small[:, 0:1]
        ss = small[:, 4:8]
        rt = small[:, 8:12]
        rstd = small[:, 12:16]
        group_exp = small[:, 48:64]
        expert_exp = small[:, 16:20]

        xn = area_a[:, :].rearrange("p (i d) -> p i d", i=NT)
        sT = area_a[:, 0:2048].rearrange("p (j s) -> p j s", j=NT)
        squares = area_a[:, 2048:4096].rearrange("p (f s) -> p f s", f=NT)
        diag = area_a[:, 0:8 * P].rearrange("p (b c) -> p b c", b=8)
        v = area_b[:, 0:2048].rearrange("p (j s) -> p j s", j=NT)
        sg = area_b[:, 2048:4096].rearrange("p (j s) -> p j s", j=NT)
        uT = area_b[:, :].rearrange("p (c s) -> p c s", c=KT)
        qT = area_c[:, 0:1024].rearrange("p (d s) -> p d s", d=2)
        kT = area_c[:, 1024:2048].rearrange("p (d s) -> p d s", d=2)
        tmp = area_c[:, 2048:4096].rearrange("p (d s) -> p d s", d=4)
        ang, turns, low, wrap = (tmp[:, n, :] for n in range(4))
        sin, cos = trig[:, 0, :], trig[:, 1, :]
        decay = area_c[:, 4096:6144].rearrange("p (h s) -> p h s", h=HEADS)
        z = area_c[:, 0:4096].rearrange("p (c s) -> p c s", c=KT)
        sig = area_c[:, 4096:5120].rearrange("p (b s) -> p b s", b=2)
        ln_root, ln_scale = sig[:, 0, :], sig[:, 1, :]
        z_sum = area_c[:, 5120:5632]
        z_squares = area_a[:, :].rearrange("p (c s) -> p c s", c=KT)
        ytile = [area_a[:, 0:2048], area_a[:, 2048:4096],
                 hT[:, 0:4, :].rearrange("p k s -> p (k s)"), hT[:, 4:8, :].rearrange("p k s -> p (k s)")]

        logits = area_b[:, 0:144].rearrange("p (i e) -> p i e", i=NT)
        le = area_b[:, 144:272].rearrange("p (i e) -> p i e", i=NT)
        eq = area_b[:, 272:400].rearrange("p (i e) -> p i e", i=NT)
        table = area_b[:, 688:688 + NBLK]
        work = area_b[:, 944:1200].rearrange("p (j e) -> p j e", j=8)
        group_hot = area_b[:, 1200:1216].rearrange("p (i g) -> p i g", i=NT)
        pick, best, second, gate = (area_b[:, 1216 + 4 * n:1220 + 4 * n] for n in range(4))
        rank, base = area_b[:, 1232:1240], area_b[:, 1240:1248]
        ranki, blki = area_b[:, 1248:1256].bitcast(I32), area_b[:, 1256:1264].bitcast(I32)
        count, blocks, upto = area_b[:, 1264:1296].bitcast(I32), area_b[:, 1296:1328], area_b[:, 1328:1360]
        logitsT = area_b[0:NG + NE, 1408:1408 + S]
        spare = [hT[:, :, :].rearrange("p k s -> p (k s)"), area_c[:, 0:SLOT], area_b[:, 0:SLOT]]
        gfin = trig[:, :, :].rearrange("p a s -> p (a s)")
        block_hot = area_c[:, 3328:3328 + 8 * NBLK].rearrange("p (j b) -> p j b", j=8)
        y_out = area_c[:, 4096:4096 + GRP * QW].rearrange("p (b c) -> p b c", b=GRP)

        y_dram = [nc.dram_tensor(f"y_dram{l}", [8 * S, QW], F32, kind="Internal").ap() for l in range(NL)]

        slot_loaded = sems("slot_loaded", NSLOT)
        x_loaded = sems("x_loaded", NT)
        const_loaded = sem("const_loaded")
        decay_loaded = sem("decay_loaded")
        par_loaded = sem("par_loaded")
        pos_loaded = sem("pos_loaded")
        gfin_loaded = sem("gfin_loaded")
        spare_loaded = [sems(f"spare_loaded{l}_", len(SPARE)) for l in range(NL)]
        y_loaded = [sems(f"y_loaded{l}_", NT) for l in range(NL)]
        out_stored = sem("out_stored")
        dve_link = sem("dve_link")
        act_link = sem("act_link")
        root_ready = sem("root_ready")
        xn_ready = sem("xn_ready")
        hT_mm = sem("hT_mm")
        hT_even = sem("hT_even")
        hT_odd = sem("hT_odd")
        hi_ready, lo_ready, tile_used = sem("hi_ready"), sem("lo_ready"), sem("tile_used")
        hThi_ready, hTlo_ready, oTlo_ready = sem("hThi_ready"), sem("hTlo_ready"), sem("oTlo_ready")
        combined = sem("combined")
        angle_ready = sem("angle_ready")
        trig_arg = sem("trig_arg")
        trig_ready = sem("trig_ready")
        sc_mm, pv_mm, tr_mm = (sem(n) for n in ("sc_mm", "pv_mm", "tr_mm"))
        rot_ready, sT_ready, on_ready, x_added = (
            sem(n) for n in ("rot_ready", "sT_ready", "on_ready", "x_added"))
        v_ready, sg_ready, oroot_ready, oT_ready = (
            sem(n) for n in ("v_ready", "sg_ready", "oroot_ready", "oT_ready"))
        act_head, dve_head, dve_norm = sem("act_head"), sem("dve_head"), sem("dve_norm")
        diag_ready, diag_used, zpe_ready, z_summed = (
            sem(n) for n in ("diag_ready", "diag_used", "zpe_ready", "z_summed"))
        sig_ready, u_ready, z_ready, mean_mm, centred, squared, var_mm, lnroot_ready, zn_ready, \
            zh_ready, pw2_mm, x2_added, pad_zero, dve_conv = (
                sem(n) for n in ("sig_ready", "u_ready", "z_ready", "mean_mm", "centred", "squared", "var_mm",
                                 "lnroot_ready", "zn_ready", "zh_ready", "pw2_mm", "x2_added", "pad_zero",
                                 "dve_conv"))
        def both(name):
            return sems(name, NL)
        wts_ready, rstd_ready, logitT_ready, logitT_mm, logit_mm, exp_arg, exp_ready, onehot_ready, rank_mm, cum_ready, spread_ready, idx_mm, idx_ready = (
            both(n) for n in ("wts_ready", "rstd_ready", "logitT_ready", "logitT_mm", "logit_mm", "exp_arg", "exp_ready", "onehot_ready", "rank_mm", "cum_ready",
                              "spread_ready", "idx_mm", "idx_ready"))
        hot_step, rows_known, pick_mm, staged = (both(n) for n in ("hot_step", "rows_known", "pick_mm", "staged"))
        scattered_lo, scattered_hi, y_free, rows_out = (
            both(n) for n in ("scattered_lo", "scattered_hi", "y_free", "rows_out"))
        idx_copied, t1_mm, hgT_ready, gu_mm, silu_ready, act_ready, t2_mm, aT_ready, \
            y_mm, y_ready = (
                both(n) for n in ("idx_copied", "t1_mm", "hgT_ready", "gu_mm",
                                  "silu_ready", "act_ready", "t2_mm", "aT_ready", "y_mm", "y_ready"))

        after_ret = [128, 64, 64, 64, 0, 0]

        def expert_base(l, s):
            early = sum(slots_of[e % 2][2] == s for e in SPARE)
            return after_ret[s] + l * (16 * (NE // 2 - early) + in_conv[s])

        slots_of = [(0, 1, 2), (3, 4, 5)]
        in_conv = [48, 48, 32, 32, 0, 0]
        ret_tiles = HEADS * 4 * TILES
        pw1_tiles = 4 * TILES

        pe_taps = [(c, k) for c in PE_CHANNELS for k in range(WIDTH)] + \
            [(SHARED, k) for k in range(WIDTH - SHARED_TAPS, WIDTH)]

        def tile_column(output, k):
            return (k % 4) * D + (k // 4) * 512 if output else k * 512

        banks_of = [(0, 4), (4, 0)]

        block = ctx.enter_context(nc.Block())

        @block.sync
        def _(sp):
            def load_columns(s, w, k, lo, n, at=0):
                dst = ring[:, s, :].rearrange("p (k c) -> p k c", k=k)[:, :, at:at + n]
                sp.dma_start(dst, w[:, bass.ds(lo, n)].rearrange("(k p) c -> p k c", p=P)) \
                    .then_inc(slot_loaded[s], 16)

            def load_rows(s, w, lo, n):
                k = n // P
                dst = ring[:, s, :].rearrange("p (k c) -> p k c", k=k)
                sp.dma_start(dst, w[bass.ds(lo, n), :].rearrange("(k p) c -> p k c", p=P)) \
                    .then_inc(slot_loaded[s], 16)

            def load_head_qk(h):
                load_columns(0, w_in, KT, h * DK, DK)
                load_columns(0, w_in, KT, h * DK + QK, DK, at=DK)

            sp.dma_start(area_b[:, 0:S].bitcast(I32), pos_in.partition_broadcast(P)).then_inc(pos_loaded, 16)
            sp.dma_start(const[:, :], const_in).then_inc(const_loaded, 16)
            for i in range(NT):
                sp.dma_start(x[:, i, :], x_in[i * P:(i + 1) * P, :]).then_inc(x_loaded[i], 16)
            load_head_qk(0)
            load_columns(1, w_in, KT, 2 * QK, DV)
            sp.dma_start(decay[:, :, :], decay_in.rearrange("h p s -> p h s")).then_inc(decay_loaded, 16)
            load_columns(2, w_in, KT, 2 * QK + RV, DV)
            load_rows(3, w_out, 0, DV)
            with sp.Fori(1, HEADS) as h:
                sp.wait_ge(lo_ready, 4 * TILES * h - 3 * TILES)
                load_head_qk(h)
                sp.wait_ge(lo_ready, 4 * TILES * h - 2 * TILES)
                load_columns(1, w_in, KT, h * DV + 2 * QK, DV)
                sp.wait_ge(lo_ready, 4 * TILES * h - TILES)
                load_columns(2, w_in, KT, h * DV + (2 * QK + RV), DV)
                sp.wait_ge(lo_ready, 4 * TILES * h)
                load_rows(3, w_out, h * DV, DV)

            def first_experts(l, tiles):
                sources = [(w_gate, 0, D), (w_up, 0, D), (w_down, 0, FF), (w_gate, 1, D), (w_up, 1, D), (w_down, 1, FF)]
                for s, (w, e, n) in enumerate(sources):
                    if s < 4:
                        sp.wait_ge(lo_ready, tiles[s])
                    elif s == 4:
                        sp.wait_ge(tile_used, NWT + tiles[4])
                    load_rows(s, w[l, e], 0, n)

            first_experts(0, [ret_tiles - n * TILES for n in (3, 2, 1, 0, 0)])

            for l in range(NL):
                gate_l = w_gate[l].rearrange("e d f -> (e d) f")
                up_l = w_up[l].rearrange("e d f -> (e d) f")
                down_l = w_down[l].rearrange("e f d -> (e f) d")
                for n, left in enumerate((logitT_mm, idx_mm, wts_ready)):
                    sp.wait_ge(left[l], 1)
                    sp.dma_start(spare[n].rearrange("p (k d) -> p k d", k=4),
                                 w_down[l, SPARE[n]].rearrange("(k p) d -> p k d", p=P)) \
                        .then_inc(spare_loaded[l][n], 16)
                if l == 1:
                    sp.dma_start(gfin, g_final.partition_broadcast(P)).then_inc(gfin_loaded, 16)
                sp.wait_ge(cum_ready[l], 1)
                sp.nop(nofuse=True)
                with sp.Fori(1, SPARE[0] // 2) as pair:
                    for odd in range(2):
                        s_gate, s_up, s_down = slots_of[odd]
                        upto = sp.value_load(cum[0:1, bass.ds(2 * pair + (odd - 1), 1)], min_val=1, max_val=NBLK - 1)
                        e = 2 * pair + odd
                        sp.wait_ge(gu_mm[l], upto)
                        load_rows(s_gate, gate_l, e * D, D)
                        load_rows(s_up, up_l, e * D, D)
                        sp.wait_ge(y_mm[l], upto)
                        load_rows(s_down, down_l, e * FF, FF)
                for e in range(SPARE[0] // 2 * 2, NE):
                    s_gate, s_up, s_down = slots_of[e % 2]
                    upto = sp.value_load(cum[0:1, e - 1:e], min_val=1, max_val=NBLK - 1)
                    sp.wait_ge(gu_mm[l], upto)
                    load_rows(s_gate, w_gate[l, e], 0, D)
                    load_rows(s_up, w_up[l, e], 0, D)
                    if e not in SPARE:
                        sp.wait_ge(y_mm[l], upto)
                        load_rows(s_down, w_down[l, e], 0, FF)
                if l == 0:
                    total = sp.value_load(cum[0:1, NE:NE + 1], min_val=NE, max_val=NBLK - 1)
                    last = sp.value_load(cum[0:1, NE - 1:NE], min_val=1, max_val=NBLK - 1)
                    for j in range(4):
                        if j == 2:
                            sp.wait_ge(y_mm[l], last)
                        else:
                            sp.wait_ge(gu_mm[l], last if j < 2 else total)
                        load_columns(j, w_pw1, KT, j * 2 * P, 2 * P)
                        load_columns(j, w_pw1, KT, j * 2 * P + D, 2 * P, at=2 * P)
                sp.wait_ge(rows_out[l], 1)
                for i in range(NT):
                    sp.dma_start(ytile[i], y_dram[l].rearrange("(t r) c -> t (r c)", r=8)[i * P:(i + 1) * P, :]) \
                        .then_inc(y_loaded[l][i], 16)
                if l == 0:
                    for n in range(2):
                        sp.wait_ge(lo_ready, ret_tiles + (n + 1) * TILES)
                        load_columns(n, w_pw2, KT, n * 512, 512)
                    split = ret_tiles + pw1_tiles
                    sp.wait_ge(lo_ready, split - TILES)
                    load_rows(2, w_down[1, 0], 0, FF)
                    sp.wait_ge(lo_ready, split)
                    load_rows(3, w_gate[1, 1], 0, D)
                    sp.wait_ge(lo_ready, split + TILES)
                    load_rows(0, w_gate[1, 0], 0, D)
                    sp.wait_ge(lo_ready, split + 2 * TILES)
                    load_rows(1, w_up[1, 0], 0, D)
                    sp.wait_ge(tile_used, NWT + split + 2 * TILES)
                    load_rows(4, w_up[1, 1], 0, D)
                    load_rows(5, w_down[1, 1], 0, FF)
            for i in range(NT):
                sp.wait_ge(xn_ready, 4 * 4 + i + 1)
                sp.dma_start(out[i * P:(i + 1) * P, :], xn[:, i, :]).then_inc(out_stored, 16)
            sp.wait_ge(out_stored, 16 * NT)

        @block.gpsimd
        def _(pool):
            def split_lo(n, place, s, at):
                pool.wait_ge(hi_ready, n + 1)
                nc.gpsimd.tensor_tensor(w_lo[:, place, :], ring[:, s, at:at + 512],
                                        w_hi[:, place, :].bitcast(F32), ALU.subtract).then_inc(lo_ready, 1)

            pool.wait_ge(angle_ready, 1)
            nc.gpsimd.tensor_scalar(sin, ang, PI, -PI, ALU.min, ALU.max).then_inc(trig_arg, 1)
            nc.gpsimd.tensor_scalar(cos, low, PI, -PI, ALU.min, ALU.max).then_inc(trig_arg, 1)

            with pool.Fori(0, HEADS) as h:
                for s in range(4):
                    for k in range(TILES):
                        split_lo(4 * TILES * h + (s * TILES + k), k % NWT, s, tile_column(s == 3, k))

            scatter_bound = pool.to_reg(8 * S - 1)

            for l in range(NL):
                def scatter(b):
                    pool.indirect_dma_start(
                        y_dram[l], bass.IndirectOffsetOnAxis(ap=idx_s[:, b:b + 1].bitcast(U32), axis=0),
                        y_out[:, b, :], None, bounds_check=scatter_bound, oob_is_err=False) \
                        .then_inc((scattered_lo if b < GRP // 2 else scattered_hi)[l], 16)

                if l == 1:
                    for n in range(pw1_tiles + 2 * TILES):
                        if n == pw1_tiles + NWT:
                            pool.wait_ge(z_ready, 2)
                            nc.gpsimd.tensor_tensor(z_sum, z[:, 0, :], z[:, 1, :], ALU.add).then_inc(z_summed, 1)
                            for m, (c, ready, count) in enumerate(((4, z_ready, 3), (5, z_ready, 4), (2, zpe_ready, 1))):
                                pool.wait_ge(ready, count)
                                pool.wait_ge(z_summed, m + 1)
                                nc.gpsimd.tensor_tensor(z_sum, z_sum, z[:, c, :], ALU.add).then_inc(z_summed, 1)
                        split_lo(ret_tiles + n, n % NWT, n // TILES % 4, tile_column(False, n % TILES))
                pool.wait_ge(idx_ready[l], 1)
                pool.sem_inc(y_free[l], GRP)
                total = pool.value_load(cum[0:1, NE:NE + 1], min_val=NE, max_val=NBLK - GRP)
                steps = pool.value_load(cum[0:1, NE + 1:NE + 2], min_val=NE // GRP - 1, max_val=NBLK // GRP - 2)
                with pool.Fori(0, steps) as g:
                    pool.tensor_copy(idx_s[:, :], idx[:, bass.ds(GRP * g, GRP)]).then_inc(idx_copied[l], 1)
                    pool.wait_ge(idx_copied[l], g + 1)
                    for b in range(GRP):
                        pool.wait_ge(y_ready[l], GRP * g + (b + 1))
                        pool.nop(nofuse=True)
                        scatter(b)
                        if b == GRP - 2:
                            pool.wait_ge(scattered_lo[l], 8 * GRP * g + 8 * GRP)
                            pool.sem_inc(y_free[l], GRP // 2)
                    pool.wait_ge(scattered_hi[l], 8 * GRP * g + 8 * GRP)
                    pool.sem_inc(y_free[l], GRP // 2)
                pool.tensor_copy(idx_s[:, :], idx[:, bass.ds(GRP * steps, GRP)]).then_inc(idx_copied[l], 1)
                pool.wait_ge(idx_copied[l], steps + 1)
                for b in range(GRP):
                    pool.wait_ge(y_ready[l], GRP * steps + (b + 1))
                    pool.nop(nofuse=True)
                    scatter(b)
                pool.wait_ge(scattered_lo[l], 8 * GRP * steps + 8 * GRP)
                pool.wait_ge(scattered_hi[l], 8 * GRP * steps + 8 * GRP)
                pool.wait_ge(pick_mm[l], total + 2)
                pool.sem_inc(rows_out[l], 1)

        @block.scalar
        def _(act):
            link = Link(act, act_link)

            def norm_roots(n, x_ready):
                for i in range(NT):
                    x_ready(i)
                    link.done(nc.scalar.activation(xn[:, i, :], x[:, i, :], ACT.Square, accum_out=ss[:, i:i + 1]))
                    nc.scalar.activation(rt[:, i:i + 1], ss[:, i:i + 1], ACT.Sqrt, bias=eps,
                                         scale=1.0 / D).then_inc(root_ready, 1)

            def split_hi(n, place, s, at):
                act.wait_ge(tile_used, n + 1)
                nc.scalar.copy(w_hi[:, place, :], ring[:, s, at:at + 512]).then_inc(hi_ready, 1)

            def norm_hi(n, m, gain):
                for k in range(KT):
                    act.wait_ge(hT_mm, KT * n + k + 1)
                    nc.scalar.activation(hT_hi[:, k, :], ps[:, k, :], ACT.Copy,
                                         scale=par[:, gain + k:gain + k + 1]).then_inc(hThi_ready, 1)

            def turned_x(n):
                for k in range(0, KT, 2):
                    act.wait_ge(hT_mm, KT * n + k + 1)
                    nc.scalar.copy(hT[:, k, :], ps[:, k, :]).then_inc(hT_even, 1)

            def expert_norm(l):
                act.wait_ge(rstd_ready[l], 1)
                for i in range(NT):
                    nc.scalar.activation(xn[:, i, :], x[:, i, :], ACT.Copy, scale=rstd[:, i:i + 1]) \
                        .then_inc(xn_ready, 1)

            def expert_blocks(l):
                act.wait_ge(exp_arg[l], 1)
                nc.scalar.activation(group_exp, group_exp, ACT.Exp).then_inc(exp_ready[l], 1)
                act.wait_ge(exp_arg[l], 2)
                nc.scalar.activation(expert_exp, expert_exp, ACT.Exp).then_inc(exp_ready[l], 1)
                act.wait_ge(cum_ready[l], 1)
                total = act.value_load(cum[0:1, NE:NE + 1], min_val=NE, max_val=NBLK - 1)
                with act.Fori(0, total) as t:
                    act.wait_ge(gu_mm[l], t + 1)
                    nc.scalar.activation(sg_e[:, :], ps[:, 2, 0:P], ACT.Silu).then_inc(silu_ready[l], 1)
                    act.wait_ge(t2_mm[l], t + 1)
                    nc.scalar.copy(aT_e[:, :], ps[:, 3, 0:P]).then_inc(aT_ready[l], 1)
                    act.wait_ge(y_mm[l], t + 1)
                    act.wait_ge(y_free[l], t + 1)
                    nc.scalar.copy(area_c[:, bass.ds((t % GRP) * QW + 4096, QW)], ps[:, 4, 0:QW]) \
                        .then_inc(y_ready[l], 1)
                act.wait_ge(y_ready[l], total)
                act.sem_inc(y_ready[l], GRP)

            act.dma_start(par[:, :], par_in).then_inc(par_loaded, 16)
            act.dma_start(wr[:, :, :, :], w_router).then_inc(par_loaded, 16)
            act.dma_start(bias_2[:, :], b_pw2).then_inc(par_loaded, 16)
            act.dma_start(bias_r[:, :, :].rearrange("p l e -> p (l e)"), b_router.partition_broadcast(P)) \
                .then_inc(par_loaded, 16)
            act.wait_ge(pad_zero, 1)
            norm_roots(0, lambda i: act.wait_ge(x_loaded[i], 16))
            act.wait_ge(trig_arg, 2)
            nc.scalar.activation(trig[:, :, :], trig[:, :, :], ACT.Sin).then_inc(trig_ready, 1)
            act.wait_ge(par_loaded, 64)
            norm_hi(0, 0, G_MIX)
            with act.Fori(0, HEADS // 2) as pair:
                for odd in range(2):
                    h, A, B = 2 * pair + odd, *banks_of[odd]

                    def split(s, first, last):
                        for k in range(first, last):
                            split_hi(4 * TILES * h + (s * TILES + k), k % NWT, s, tile_column(s == 3, k))

                    act.wait_ge(slot_loaded[0], 32 * h + 32)
                    split(0, 0, TILES)
                    act.wait_ge(slot_loaded[1], 16 * h + 16)
                    split(1, 0, TILES)
                    act.wait_ge(slot_loaded[2], 16 * h + 16)
                    split(2, 0, NWT)
                    act.wait_ge(tile_used, 4 * TILES * h + (2 * TILES + NWT))
                    for i in range(NT):
                        nc.scalar.copy(v[:, i, :], ps[:, B + i, :]).then_inc(v_ready, 1)
                    split(2, NWT, TILES)
                    act.wait_ge(slot_loaded[3], 16 * h + 16)
                    split(3, 0, NWT)
                    act.wait_ge(tile_used, 4 * TILES * h + (3 * TILES + NWT))
                    for i in range(NT):
                        nc.scalar.activation(sg[:, i, :], ps[:, A + i, :], ACT.Silu).then_inc(sg_ready, 1)
                    for i in range(NT):
                        act.wait_ge(pv_mm, 4 * h + (i + 1))
                        nc.scalar.activation(squares[:, i, :], ps[:, B + i, :], ACT.Square,
                                             accum_out=ss[:, i:i + 1]).then_inc(act_head, 1)
                        act.wait_ge(act_head, 4 * h + (i + 1))
                        nc.scalar.activation(rt[:, i:i + 1], ss[:, i:i + 1], ACT.Sqrt, bias=eps,
                                             scale=1.0 / DV).then_inc(oroot_ready, 1)
                    for f in range(NT):
                        act.wait_ge(tr_mm, 4 * h + (f + 1))
                        nc.scalar.activation(oT_hi[:, f, :], ps[:, A + f, :], ACT.Copy,
                                             scale=par[:, bass.ds(4 * h + (G_HEAD + f), 1)]).then_inc(oT_ready, 1)
                    split(3, NWT, TILES)
            turned_x(1)
            norm_roots(1, lambda i: act.wait_ge(x_added, 8 * HEADS + 8))
            expert_norm(0)
            expert_blocks(0)

            norm_roots(2, lambda i: act.wait_ge(combined, i + 1))
            norm_hi(2, 1, G_MIX + KT)

            def split_conv(first, last):
                for n in range(first, last):
                    if n % TILES == 0:
                        s = n // TILES % 4
                        act.wait_ge(slot_loaded[s], expert_base(1, s) - in_conv[s] + (32 if n < pw1_tiles else 48))
                    split_hi(ret_tiles + n, n % NWT, n // TILES % 4, tile_column(False, n % TILES))

            split_conv(0, TILES)
            for j in range(4):
                split_conv((j + 1) * TILES, (j + 1) * TILES + NWT)
                act.wait_ge(tile_used, ret_tiles + (j + 1) * TILES + NWT)
                for c in (2 * j, 2 * j + 1):
                    if c >= 2:
                        act.wait_ge(u_ready, c - 1)
                    nc.scalar.activation(sig[:, c % 2, :], ps[:, 4 * (j % 2) + 2 + c % 2, :], ACT.Sigmoid,
                                         bias=par[:, B_PW1 + KT + c:B_PW1 + KT + c + 1]).then_inc(sig_ready, 1)
                if j < 3:
                    split_conv((j + 1) * TILES + NWT, (j + 2) * TILES)
            def convolved(n):
                c = PE_CHANNELS[n]
                act.wait_ge(diag_used, (n + 1) * WIDTH)
                nc.scalar.activation(z[:, c, :], ps[:, n, :], ACT.Identity,
                                     bias=par[:, B_DW + c:B_DW + c + 1]).then_inc(zpe_ready, 1)

            for n, (c, k) in enumerate(pe_taps):
                if n == WIDTH + 7:
                    convolved(0)
                if n >= 8:
                    act.wait_ge(diag_used, n - 7)
                nc.scalar.activation(diag[:, n % 8, :], ident, ACT.Copy,
                                     scale=par[:, W_DW + c * WIDTH + k:W_DW + c * WIDTH + k + 1]) \
                    .then_inc(diag_ready, 1)
            convolved(1)
            for c in range(KT):
                act.wait_ge(centred, c + 1)
                nc.scalar.activation(z_squares[:, c, :], z[:, c, :], ACT.Square).then_inc(squared, 1)
            act.wait_ge(var_mm, 1)
            nc.scalar.activation(ln_root, ps[:, 3, :], ACT.Sqrt, bias=eps, scale=1.0 / D).then_inc(lnroot_ready, 1)
            for k in range(KT):
                act.wait_ge(zn_ready, k + 1)
                nc.scalar.activation(z[:, k, :], z[:, k, :], ACT.Silu, bias=par[:, LN_B + k:LN_B + k + 1],
                                     scale=par[:, LN_G + k:LN_G + k + 1]).then_inc(zh_ready, 1)
                act.wait_ge(zh_ready, k + 1)
                nc.scalar.copy(hT_hi[:, k, :], z[:, k, :]).then_inc(hThi_ready, 1)
            split_conv(pw1_tiles + NWT, pw1_tiles + 2 * TILES)
            turned_x(3)
            norm_roots(3, lambda i: act.wait_ge(x2_added, NT + i + 1))
            expert_norm(1)
            expert_blocks(1)
            norm_roots(4, lambda i: act.wait_ge(combined, NT + i + 1))

        @block.tensor
        def _(pe):
            def turn_norm(n):
                for i in range(NT):
                    pe.wait_ge(xn_ready, 4 * n + i + 1)
                    for k in range(KT):
                        last = nc.tensor.transpose(ps[:, k, i * P:(i + 1) * P], xn[:, i, k * P:(k + 1) * P], ident)
                        if i == NT - 1:
                            last.then_inc(hT_mm, 1)

            def turn_x(added, count):
                for k in range(KT):
                    for i in range(NT):
                        if k == 0:
                            pe.wait_ge(added, count - NT)
                        elif k == KT // 2:
                            pe.wait_ge(added, count - NT + i + 1)
                        last = nc.tensor.transpose(ps[:, k, i * P:(i + 1) * P], x[:, i, k * P:(k + 1) * P], ident)
                    last.then_inc(hT_mm, 1)

            def three(at, lhs, rhs, start, stop):
                nc.tensor.matmul(at, lhs[0], rhs[0], start=start, stop=False)
                nc.tensor.matmul(at, lhs[0], rhs[1], start=False, stop=False)
                return nc.tensor.matmul(at, lhs[1], rhs[0], start=False, stop=stop)

            def product(number, bank, weights_stand, operand=None, begin=True, last=True, tiles=range(TILES),
                        split=None, turned=None):
                tokens = operand or (hT_hi, hT_lo)
                for k in tiles:
                    w = (w_hi[:, k % NWT, :], w_lo[:, k % NWT, :])
                    pe.wait_ge(lo_ready, number(k) + 1)
                    if split is not None:
                        pe.wait_ge(hThi_ready, split[0] + k + 1)
                        pe.wait_ge(hTlo_ready, split[0] + max(k + 1, split[1]))
                    if turned is not None:
                        pe.wait_ge(oT_ready, turned + (k + 1))
                        pe.wait_ge(oTlo_ready, turned + (k + 1))
                    row = k % 4 if operand else k
                    for m in range(4):
                        cols = slice(m * P, (m + 1) * P)
                        start, stop = begin and k == tiles[0], last and k == tiles[-1]
                        if weights_stand:
                            ins = three(ps[:, bank + m, :], [t[:, cols] for t in w], [t[:, row, :] for t in tokens],
                                        start, stop)
                        else:
                            ins = three(ps[:, bank + m, :], [t[:, row, cols] for t in tokens], w, start, stop)
                    ins.then_inc(tile_used, 1)

            def pick_rows(l, t):
                pe.wait_ge(rows_known[l], t + 1)
                if not (isinstance(t, int) and t == 0):
                    pe.wait_ge(staged[l], t)
                for i in range(NT):
                    for g in range(4):
                        last = nc.tensor.matmul(ps[32 * g:32 * g + 32, 6, 0:QW], block_rows[:, i, :],
                                                xn[:, i, g * QW:(g + 1) * QW],
                                                start=(i == 0), stop=(i == NT - 1), tile_position=(0, 32 * g))
                last.then_inc(pick_mm[l], 1)

            def turn_block(l, t):
                pe.wait_ge(staged[l], t + 1)
                for c in range(2):
                    last = nc.tensor.transpose(ps[:, 1, c * P:(c + 1) * P], hg[:, c * P:(c + 1) * P], ident)
                last.then_inc(t1_mm[l], 1)

            def route(l):
                for k in range(KT):
                    pe.wait_ge(hT_odd if k % 2 else hT_even, 4 * l + k // 2 + 1)
                    last = nc.tensor.matmul(ps[0:NG + NE, 0, :], wr[:, l, k, :], hT[:, k, :],
                                            start=(k == 0), stop=(k == KT - 1))
                last.then_inc(logitT_mm[l], 1)
                pe.wait_ge(logitT_ready[l], 1)
                for i in range(NT):
                    last = nc.tensor.transpose(ps[:, 1, i * 64:i * 64 + NG + NE], logitsT[:, i * P:(i + 1) * P],
                                               ident[0:NG + NE, 0:NG + NE])
                last.then_inc(logit_mm[l], 1)
                pe.wait_ge(onehot_ready[l], 1)
                nc.tensor.matmul(ps[:, 5, 0:9 * NE], counting[:, 0, :], onehot_r[:, :], start=True, stop=False)
                for j in range(8):
                    last = nc.tensor.matmul(
                        ps[:, 5, (j + 1) * NE:9 * NE].rearrange("p (r e) -> p r e", e=NE), counting[:, 1, :],
                        onehot_r[:, j * NE:(j + 1) * NE].unsqueeze(1).to_broadcast([P, 8 - j, NE]),
                        start=False, stop=(j == 7))
                last.then_inc(rank_mm[l], 1)
                for i in range(NT):
                    pe.wait_ge(xn_ready, 4 * (2 * l + 1) + i + 1)
                pick_rows(l, 0)
                turn_block(l, 0)
                pick_rows(l, 1)
                pe.wait_ge(spread_ready[l], 1)
                for j in range(8):
                    last = nc.tensor.matmul(ps[:, 7, 0:NBLK], slot_hot_r[:, j, :], block_hot_r[:, j, :],
                                            start=(j == 0), stop=(j == 7))
                last.then_inc(idx_mm[l], 1)

            def one_block(l, t, pair, s_gate, s_up, s_down, early=None):
                gate_up = ring[:, s_gate:s_gate + 2, :].rearrange("p w (k f) -> p w k f", k=KT)
                down = (ring[:, s_down, :] if early is None else spare[early]).rearrange("p (k d) -> p k d", k=4)
                pe.wait_ge(hgT_ready[l], t + 1)
                for s in (s_gate, s_up):
                    pe.wait_ge(slot_loaded[s], 16 * pair + (expert_base(l, s) + 16))
                for k in range(KT):
                    for g in range(4):
                        last = nc.tensor.matmul(ps[32 * g:32 * g + 32, 2, 0:256], hgT[:, k, :],
                                                gate_up[:, :, k, g * P:(g + 1) * P],
                                                start=(k == 0), stop=(k == KT - 1), tile_position=(0, 32 * g))
                last.then_inc(gu_mm[l], 1)
                pick_rows(l, t + 2)
                pe.wait_ge(act_ready[l], t + 1)
                nc.tensor.transpose(ps[:, 3, 0:P], a_e[:, :], ident).then_inc(t2_mm[l], 1)
                turn_block(l, t + 1)
                pe.wait_ge(aT_ready[l], t + 1)
                if early is None:
                    pe.wait_ge(slot_loaded[s_down], 16 * pair + (expert_base(l, s_down) + 16))
                else:
                    pe.wait_ge(spare_loaded[l][early], 16)
                for k in range(4):
                    for g in range(4):
                        last = nc.tensor.matmul(ps[32 * g:32 * g + 32, 4, 0:256], aT_e[:, k * BLK:(k + 1) * BLK],
                                                down[:, k, g * 256:(g + 1) * 256],
                                                start=(k == 0), stop=(k == 3), tile_position=(0, 32 * g))
                last.then_inc(y_mm[l], 1)

            def experts(l):
                with pe.Fori(0, SPARE[0] // 2) as pair:
                    for odd in range(2):
                        slots = slots_of[odd]
                        first = pe.value_load(cum[0:1, bass.ds(2 * pair + odd, 1)], min_val=0, max_val=NBLK - 2)
                        after = pe.value_load(cum[0:1, bass.ds(2 * pair + (odd + 1), 1)], min_val=1, max_val=NBLK - 1)
                        with pe.Fori(first, after) as t:
                            one_block(l, t, pair, *slots)
                for e in range(SPARE[0] // 2 * 2, NE):
                    first = pe.value_load(cum[0:1, e:e + 1], min_val=0, max_val=NBLK - 2)
                    after = pe.value_load(cum[0:1, e + 1:e + 2], min_val=1, max_val=NBLK - 1)
                    with pe.Fori(first, after) as t:
                        one_block(l, t, e // 2, *slots_of[e % 2], early=SPARE.index(e) if e in SPARE else None)

            pe.sem_inc(tile_used, NWT)
            pe.wait_ge(const_loaded, 16)
            turn_norm(0)
            with pe.Fori(0, HEADS // 2) as pair:
                for odd in range(2):
                    h, A, B = 2 * pair + odd, *banks_of[odd]

                    def tile(s):
                        return lambda k: 4 * TILES * h + (s * TILES + k)

                    pe.wait_ge(x_added, 8 * h + 4)
                    product(tile(0), A, True, split=(0, 4))
                    pe.wait_ge(x_added, 8 * h + 8)
                    product(tile(1), B, False)
                    pe.wait_ge(rot_ready, 4 * h + 4)
                    product(tile(2), A, False, last=False, tiles=range(TILES // 2))
                    for j in range(NT):
                        pe.wait_ge(v_ready, 4 * h + (j + 1))
                        for d in range(2):
                            last = nc.tensor.matmul(ps[:, B + j, 0:S - j * P], kT[:, d, j * P:(j + 1) * P],
                                                    qT[:, d, j * P:S], start=(d == 0), stop=(d == 1))
                        last.then_inc(sc_mm, 1)
                    product(tile(2), A, False, begin=False, tiles=range(TILES // 2, TILES))
                    pe.wait_ge(sT_ready, 4 * h + 4)
                    for i in range(NT):
                        for j in range(i + 1):
                            last = nc.tensor.matmul(ps[:, B + i, :], sT[:, j, i * P:(i + 1) * P], v[:, j, :],
                                                    start=(j == 0), stop=(j == i))
                        last.then_inc(pv_mm, 1)
                    for i in range(NT):
                        pe.wait_ge(on_ready, 4 * h + (i + 1))
                        if i == 0:
                            pe.wait_ge(sg_ready, 4 * h + 4)
                        for f in range(NT):
                            last = nc.tensor.transpose(ps[:, A + f, i * P:(i + 1) * P], sg[:, i, f * P:(f + 1) * P],
                                                       ident)
                            if i == NT - 1:
                                last.then_inc(tr_mm, 1)
                    for n, at in enumerate((B, A)):
                        if n:
                            pe.wait_ge(oTlo_ready, 4 * h + 4)
                        product(tile(3), at, False, operand=(oT_hi, oT_lo), tiles=range(4 * n, 4 * n + 4),
                                turned=(4 * h if n == 0 else None))
            turn_x(x_added, 8 * HEADS + 8)
            route(0)
            experts(0)

            turn_norm(2)
            for j in range(4):
                if j >= 2:
                    pe.wait_ge(u_ready, 2 * j - 2)
                product(lambda k: ret_tiles + j * TILES + k, 4 * (j % 2), True, split=(KT, 4))
            bank_of = {PE_CHANNELS[0]: 0, PE_CHANNELS[1]: 1, SHARED: 3}
            pe.wait_ge(u_ready, 6)
            for n, (c, k) in enumerate(pe_taps):
                if n == len(PE_CHANNELS) * WIDTH:
                    pe.wait_ge(u_ready, SHARED + 1)
                pe.wait_ge(diag_ready, n + 1)
                nc.tensor.matmul(ps[:, bank_of[c], :], diag[:, n % 8, :], uT[:, c, k:k + S],
                                 start=(k == 0 or k == WIDTH - SHARED_TAPS and c == SHARED),
                                 stop=(k == WIDTH - 1)).then_inc(diag_used, 1)
            parts = ((z_sum, z_summed, 4), (z[:, 3, :], zpe_ready, 2), (z[:, 6, :], z_ready, 5), (z[:, 7, :], z_ready, 6))
            for n, (part, ready, count) in enumerate(parts):
                pe.wait_ge(ready, count)
                last = nc.tensor.matmul(ps[:, 2, :], ones, part, start=(n == 0), stop=(n == len(parts) - 1))
            last.then_inc(mean_mm, 1)
            for c in range(KT):
                pe.wait_ge(squared, c + 1)
                last = nc.tensor.matmul(ps[:, 3, :], ones, z_squares[:, c, :], start=(c == 0), stop=(c == KT - 1))
            last.then_inc(var_mm, 1)
            pe.wait_ge(u_ready, KT)
            for n in range(2):
                product(lambda k: ret_tiles + pw1_tiles + n * TILES + k, 4 * n, False, last=False,
                        split=(2 * KT, 0))
                for i in range(NT):
                    nc.tensor.matmul(ps[:, 4 * n + i, :], const[0:1, C_ONE:C_ONE + P], bias_2[:, n * 512:(n + 1) * 512],
                                     start=False, stop=True).then_inc(pw2_mm, 1)
            turn_x(x2_added, 2 * NT)
            route(1)
            experts(1)

        @block.vector
        def _(dve):
            link = Link(dve, dve_link)
            V = nc.vector

            def scale_norm(n, tiles=range(NT)):
                for i in tiles:
                    dve.wait_ge(root_ready, 4 * n + i + 1)
                    link.done(V.reciprocal(rstd[:, i:i + 1], rt[:, i:i + 1]))
                    if n < 4:
                        V.tensor_scalar(xn[:, i, :], x[:, i, :], rstd[:, i:i + 1], None, ALU.mult) \
                            .then_inc(xn_ready, 1)
                    else:
                        V.scalar_tensor_tensor(out=xn[:, i, :], in0=x[:, i, :], scalar=rstd[:, i:i + 1],
                                               in1=gfin[:, :], op0=ALU.mult, op1=ALU.mult).then_inc(xn_ready, 1)

            def turned_x(n):
                for k in range(1, KT, 2):
                    dve.wait_ge(hT_mm, KT * n + k + 1)
                    V.tensor_copy(hT[:, k, :], ps[:, k, :]).then_inc(hT_odd, 1)

            def expert_norm(l, n):
                dve.wait_ge(root_ready, 4 * n + NT)
                V.reciprocal(rstd[:, :], rt[:, :]).then_inc(rstd_ready[l], 1)

            def norm_lo(n, m, gain):
                for k in range(KT):
                    dve.wait_ge(hThi_ready, KT * m + k + 1)
                    V.scalar_tensor_tensor(out=hT_lo[:, k, :], in0=ps[:, k, :], scalar=par[:, gain + k:gain + k + 1],
                                           in1=hT_hi[:, k, :].bitcast(F32), op0=ALU.mult, op1=ALU.subtract) \
                        .then_inc(hTlo_ready, 1)

            def first_max(l, scores, best, rev, n, oh, ready=None):
                shape = [P, NT, n]
                link.done(V.tensor_tensor(eq[:, :, 0:n], scores, best.unsqueeze(2).to_broadcast(shape), ALU.is_equal))
                link.done(V.tensor_tensor(eq[:, :, 0:n], eq[:, :, 0:n], rev.unsqueeze(1).to_broadcast(shape), ALU.mult))
                link.done(V.tensor_reduce(pick[:, :], eq[:, :, 0:n], AX, ALU.max))
                ins = V.tensor_tensor(oh, eq[:, :, 0:n], pick[:, :].unsqueeze(2).to_broadcast(shape), ALU.is_equal)
                if ready is None:
                    link.done(ins)
                else:
                    ins.then_inc(ready, 1)

            def know_rows(l, t):
                first = isinstance(t, int) and t == 0
                if not first:
                    dve.wait_ge(rows_known[l], t)
                    dve.wait_ge(pick_mm[l], t)
                dve.wait_ge(hot_step[l], 2 * t + 1)
                V.tensor_tensor(both_hot[:, :, :], const[:, C_MOD:C_MOD + BLK].unsqueeze(1).to_broadcast([P, 8, BLK]),
                                pos[:, :].unsqueeze(2).to_broadcast([P, 8, BLK]), ALU.is_equal) \
                    .then_inc(hot_step[l], 1)
                dve.wait_ge(hot_step[l], 2 * t + 2)
                V.tensor_tensor(block_rows[:, :, :], both_hot[:, 0:NT, :], both_hot[:, NT:2 * NT, :], ALU.add) \
                    .then_inc(rows_known[l], 1)
                V.tensor_scalar(pos[:, :], pos[:, :], -float(BLK), None, ALU.add).then_inc(hot_step[l], 1)

            def turned_block(l, t, gain):
                dve.wait_ge(t1_mm[l], t + 1)
                for c in range(2):
                    ins = V.tensor_tensor(
                        hgT[:, :, :].rearrange("p (q c) s -> p c q s", c=2)[:, c],
                        ps[:, 1, c * P:(c + 1) * P].rearrange("p (q s) -> p q s", q=4),
                        par[:, gain:gain + KT].rearrange("p (q c) -> p c q", c=2)[:, c].unsqueeze(2)
                        .to_broadcast([P, 4, BLK]), ALU.mult)
                ins.then_inc(hgT_ready[l], 1)

            def stage(l, t):
                if not (isinstance(t, int) and t == 0):
                    dve.wait_ge(t1_mm[l], t)
                dve.wait_ge(pick_mm[l], t + 1)
                V.tensor_copy(hg[:, :], ps[:, 6, 0:QW]).then_inc(staged[l], 1)

            def route(l, gain):
                dve.wait_ge(logitT_mm[l], 1)
                V.tensor_copy(logitsT, ps[0:NG + NE, 0, :]).then_inc(logitT_ready[l], 1)
                dve.wait_ge(logit_mm[l], 1)
                dve.wait_ge(rstd_ready[l], 1)
                for i in range(NT):
                    link.sent(V.scalar_tensor_tensor(out=logits[:, i, :], in0=ps[:, 1, i * 64:i * 64 + NG + NE],
                                                     scalar=rstd[:, i:i + 1], in1=bias_r[:, l, :],
                                                     op0=ALU.mult, op1=ALU.add))
                link.wait()
                lg = logits[:, :, 0:NG]
                link.done(V.tensor_reduce(best[:, :], lg, AX, ALU.max))
                V.tensor_tensor(group_exp.rearrange("p (i g) -> p i g", i=NT), lg,
                                best[:, :].unsqueeze(2).to_broadcast([P, NT, NG]), ALU.subtract) \
                    .then_inc(exp_arg[l], 1)
                first_max(l, lg, best[:, :], const[:, C_REV4:C_REV4 + NG], NG, group_hot[:, :, :])
                link.done(V.tensor_scalar(group_hot[:, :, :], group_hot[:, :, :], -1.0, FAR, ALU.add, ALU.mult))
                for i in range(NT):
                    link.sent(V.tensor_tensor(
                        le[:, i, :].rearrange("p (g e) -> p g e", g=NG),
                        logits[:, i, NG:NG + NE].rearrange("p (g e) -> p g e", g=NG),
                        group_hot[:, i, :].unsqueeze(2).to_broadcast([P, NG, NPG]), ALU.add))
                link.wait()
                rev = const[:, C_REV32:C_REV32 + NE]
                oh_r = onehot_r[:, 0:8 * NE].rearrange("p (j e) -> p j e", j=8)
                oh = oh_r.bitcast(F32)
                link.sent(V.tensor_scalar(onehot_r[:, 8 * NE:9 * NE], const[:, C_ONE:C_ONE + NE], 0.0, None, ALU.mult))
                link.done(V.tensor_reduce(best[:, :], le[:, :, :], AX, ALU.max))
                first_max(l, le[:, :, :], best[:, :], rev, NE, oh_r[:, 0:NT, :])
                link.done(V.scalar_tensor_tensor(out=le[:, :, :], in0=oh[:, 0:NT, :], scalar=-3.0 * FAR,
                                                 in1=le[:, :, :], op0=ALU.mult, op1=ALU.add))
                link.done(V.tensor_reduce(second[:, :], le[:, :, :], AX, ALU.max))
                V.tensor_tensor(expert_exp, second[:, :], best[:, :], ALU.subtract).then_inc(exp_arg[l], 1)
                first_max(l, le[:, :, :], second[:, :], rev, NE, oh_r[:, NT:2 * NT, :], onehot_ready[l])
                dve.wait_ge(rank_mm[l], 1)
                link.done(V.tensor_scalar(count[:, :], ps[:, 5, 8 * NE:9 * NE], BLK - 1.0, None, ALU.add))
                link.done(V.tensor_single_scalar(count[:, :], count[:, :], 5, ALU.arith_shift_right))
                link.done(V.tensor_scalar(blocks[:, :], count[:, :], 1.0, None, ALU.max))
                link.done(V.tensor_tensor_scan(upto[:, :], blocks[:, :], blocks[:, :], 0.0, ALU.add, ALU.bypass))
                link.sent(V.tensor_copy(cum[:, 1:NE + 1], upto[:, :]))
                link.done(V.tensor_scalar(count[:, 0:1], upto[:, NE - 1:NE], -1.0, None, ALU.add))
                V.tensor_single_scalar(cum[:, NE + 1:NE + 2], count[:, 0:1], 3, ALU.arith_shift_right) \
                    .then_inc(cum_ready[l], 1)
                link.done(V.tensor_tensor(upto[:, :], upto[:, :], blocks[:, :], ALU.subtract))
                rank3 = ps[:, 5, 0:8 * NE].rearrange("p (j e) -> p j e", j=8)
                link.done(V.tensor_tensor(work[:, :, :], rank3, oh, ALU.mult))
                link.done(V.tensor_reduce(rank[:, :], work[:, :, :], AX, ALU.add))
                link.done(V.tensor_tensor(work[:, :, :], oh, upto[:, :].unsqueeze(1).to_broadcast([P, 8, NE]), ALU.mult))
                link.done(V.tensor_reduce(base[:, :], work[:, :, :], AX, ALU.add))
                V.scalar_tensor_tensor(out=pos[:, :], in0=base[:, :], scalar=float(BLK), in1=rank[:, :],
                                       op0=ALU.mult, op1=ALU.add).then_inc(hot_step[l], 1)
                know_rows(l, 0)
                link.done(V.tensor_copy(ranki[:, :], rank[:, :]))
                link.done(V.tensor_single_scalar(blki[:, :], ranki[:, :], 5, ALU.arith_shift_right))
                link.done(V.tensor_single_scalar(ranki[:, :], ranki[:, :], BLK - 1, ALU.bitwise_and))
                link.done(V.tensor_copy(rank[:, :], ranki[:, :]))
                link.done(V.tensor_tensor(base[:, :], base[:, :], blki[:, :], ALU.add))
                link.sent(V.tensor_tensor(block_hot[:, :, :],
                                          const[:, C_IOTA:C_IOTA + NBLK].unsqueeze(1).to_broadcast([P, 8, NBLK]),
                                          base[:, :].unsqueeze(2).to_broadcast([P, 8, NBLK]), ALU.is_equal))
                stage(l, 0)
                know_rows(l, 1)
                turned_block(l, 0, gain)
                link.sent(V.tensor_tensor(slot_hot_r[:, :, :],
                                          const[:, C_MOD:C_MOD + P].unsqueeze(1).to_broadcast([P, 8, P]),
                                          rank[:, :].unsqueeze(2).to_broadcast([P, 8, P]), ALU.is_equal))
                link.wait()
                V.tensor_tensor(block_hot_r[:, :, :], block_hot[:, :, :],
                                const[:, C_A:C_A + 8].unsqueeze(2).to_broadcast([P, 8, NBLK]), ALU.mult) \
                    .then_inc(spread_ready[l], 1)
                stage(l, 1)
                know_rows(l, 2)
                dve.wait_ge(idx_mm[l], 1)
                link.done(V.tensor_scalar(table, ps[:, 7, 0:NBLK], 0.0, BIG, ALU.is_equal, ALU.mult))
                link.done(V.tensor_tensor(table, table, ps[:, 7, 0:NBLK], ALU.add))
                V.tensor_scalar(idx[:, :], table, 4.0, const[:, C_QOFF:C_QOFF + 1],
                                ALU.mult, ALU.add).then_inc(idx_ready[l], 1)
                dve.wait_ge(exp_ready[l], 2)
                link.done(V.tensor_reduce(gate[:, :], group_exp.rearrange("p (i g) -> p i g", i=NT), AX, ALU.add))
                link.done(V.reciprocal(gate[:, :], gate[:, :]))
                link.done(V.tensor_scalar(second[:, :], expert_exp, 1.0, None, ALU.add))
                link.done(V.reciprocal(second[:, :], second[:, :]))
                link.done(V.tensor_tensor(wts[:, 0, :], second[:, :], gate[:, :], ALU.mult))
                V.tensor_tensor(wts[:, 1, :], wts[:, 0, :], expert_exp, ALU.mult).then_inc(wts_ready[l], 1)

            def expert_blocks(l, gain):
                total = dve.value_load(cum[0:1, NE:NE + 1], min_val=NE, max_val=NBLK - 1)
                with dve.Fori(0, total) as t:
                    dve.wait_ge(silu_ready[l], t + 1)
                    V.tensor_tensor(a_e[:, :], sg_e[:, :], ps[:, 2, P:2 * P], ALU.mult).then_inc(act_ready[l], 1)
                    dve.wait_ge(gu_mm[l], t + 1)
                    turned_block(l, t + 1, gain)
                    stage(l, t + 2)
                    know_rows(l, t + 3)

            def combine(l, n):
                dve.wait_ge(wts_ready[l], 1)
                for i in range(NT):
                    dve.wait_ge(y_loaded[l][i], 16)
                    for k in range(2):
                        ins = V.scalar_tensor_tensor(out=x[:, i, :], in0=ytile[i][:, k * D:(k + 1) * D],
                                                     scalar=wts[:, k, i:i + 1], in1=x[:, i, :],
                                                     op0=ALU.mult, op1=ALU.add)
                        if k == 0:
                            link.done(ins)
                    ins.then_inc(combined, 1)
                    if i > 0:
                        scale_norm(n, [i - 1])
                scale_norm(n, [NT - 1])

            V.memset(small[:, 0:4], EPS).then_inc(pad_zero, 1)
            link.done(V.memset(cum[:, 0:1], 0))
            dve.wait_ge(const_loaded, 16)
            dve.wait_ge(pos_loaded, 16)
            link.done(V.tensor_copy(ang, area_b[:, 0:S].bitcast(I32)))
            link.done(V.tensor_scalar(ang, ang, const[:, C_INV:C_INV + 1], None, ALU.mult))
            link.done(V.tensor_scalar(turns, ang, 1.0 / TWO_PI, ROUND, ALU.mult, ALU.add))
            link.done(V.tensor_scalar(turns, turns, ROUND, None, ALU.subtract))
            for n, part in enumerate(TURN):
                ins = V.scalar_tensor_tensor(out=ang, in0=turns, scalar=-part, in1=ang, op0=ALU.mult, op1=ALU.add)
                if n < 2:
                    link.done(ins)
            link.done(ins)
            link.done(V.tensor_scalar(low, ang, TWO_PI / 4, None, ALU.add))
            link.done(V.tensor_scalar(wrap, low, PI, -TWO_PI, ALU.is_gt, ALU.mult))
            V.tensor_tensor(low, low, wrap, ALU.add).then_inc(angle_ready, 1)
            scale_norm(0)
            dve.wait_ge(par_loaded, 64)
            norm_lo(0, 0, G_MIX)
            V.sem_inc(x_added, 8)
            for n, at in enumerate((C_TRI, C_ONE)):
                link.sent(V.tensor_copy(counting[:, n, :], const[:, at:at + P]))
            for l in range(NL):
                gains = par[:, G_FFN + KT * l:G_FFN + KT * (l + 1)].unsqueeze(2).to_broadcast([P, KT, NG + NE])
                link.done(V.tensor_tensor(wr[:, l], wr[:, l], gains, ALU.mult))
            dve.wait_ge(trig_ready, 1)
            dve.wait_ge(decay_loaded, 16)
            with dve.Fori(0, HEADS // 2) as pair:
                for odd in range(2):
                    h, A, B = 2 * pair + odd, *banks_of[odd]
                    for n, dst in enumerate((qT, kT)):
                        lo, hi = ps[:, A + 2 * n, :], ps[:, A + 2 * n + 1, :]
                        if n == 0:
                            dve.wait_ge(tile_used, 4 * TILES * h + (TILES + NWT))
                        if n == 1:
                            dve.wait_ge(rot_ready, 4 * h + 2)
                        V.tensor_tensor(tmp[:, 0, :], lo, cos, ALU.mult)
                        V.tensor_tensor(tmp[:, 1, :], hi, sin, ALU.mult)
                        V.tensor_tensor(tmp[:, 2, :], lo, sin, ALU.mult)
                        V.tensor_tensor(tmp[:, 3, :], hi, cos, ALU.mult).then_inc(dve_head, 1)
                        dve.wait_ge(dve_head, 2 * h + (n + 1))
                        V.tensor_tensor(dst[:, 0, :], tmp[:, 0, :], tmp[:, 1, :], ALU.subtract).then_inc(rot_ready, 1)
                        V.tensor_tensor(dst[:, 1, :], tmp[:, 2, :], tmp[:, 3, :], ALU.add).then_inc(rot_ready, 1)
                    for j in range(NT):
                        dve.wait_ge(sc_mm, 4 * h + (j + 1))
                        V.tensor_tensor(sT[:, j, j * P:S], ps[:, B + j, 0:S - j * P],
                                        decay[:, bass.ds(h, 1), 0:S - j * P].rearrange("p a s -> p (a s)"),
                                        ALU.mult).then_inc(sT_ready, 1)
                    for i in range(NT):
                        dve.wait_ge(oroot_ready, 4 * h + (i + 1))
                        V.reciprocal(rstd[:, i:i + 1], rt[:, i:i + 1]).then_inc(dve_norm, 1)
                        dve.wait_ge(dve_norm, 4 * h + (i + 1))
                        dve.wait_ge(sg_ready, 4 * h + (i + 1))
                        V.scalar_tensor_tensor(out=sg[:, i, :], in0=ps[:, B + i, :], scalar=rstd[:, i:i + 1],
                                               in1=sg[:, i, :], op0=ALU.mult, op1=ALU.mult).then_inc(on_ready, 1)
                    for f in range(NT):
                        dve.wait_ge(oT_ready, 4 * h + (f + 1))
                        V.scalar_tensor_tensor(out=oT_lo[:, f, :], in0=ps[:, A + f, :],
                                               scalar=par[:, bass.ds(4 * h + (G_HEAD + f), 1)],
                                               in1=oT_hi[:, f, :].bitcast(F32), op0=ALU.mult, op1=ALU.subtract) \
                            .then_inc(oTlo_ready, 1)
                    for m in range(8):
                        i, n = m % 4, m // 4
                        if i == 0:
                            dve.wait_ge(tile_used, 4 * TILES * h + (3 * TILES + 4 * (n + 1) + NWT))
                        V.tensor_tensor(x[:, i, n * 512:(n + 1) * 512], x[:, i, n * 512:(n + 1) * 512], ps[:, (A if n else B) + i, :],
                                        ALU.add).then_inc(x_added, 1)
            dve.wait_ge(x_added, 8 * HEADS + 8)
            turned_x(1)
            expert_norm(0, 1)
            route(0, G_FFN)
            expert_blocks(0, G_FFN)
            combine(0, 2)

            norm_lo(2, 1, G_MIX + KT)
            link.done(V.memset(uT[:, :, 0:PAD], 0.0))

            def glu(j):
                for c in (2 * j, 2 * j + 1):
                    dve.wait_ge(sig_ready, c + 1)
                    V.scalar_tensor_tensor(out=uT[:, c, PAD:PAD + S], in0=ps[:, 4 * (j % 2) + c % 2, :],
                                           scalar=par[:, B_PW1 + c:B_PW1 + c + 1], in1=sig[:, c % 2, :],
                                           op0=ALU.add, op1=ALU.mult).then_inc(u_ready, 1)

            glu(0)
            taps = 0
            for pair, channels in enumerate(zip(DVE_CHANNELS[::2], DVE_CHANNELS[1::2])):
                dve.wait_ge(u_ready, (2, 6, 8)[pair])
                last = [0, 0]
                for k in range(WIDTH):
                    if pair == 0 and k == 12:
                        glu(1)
                    if pair == 0 and k == 28:
                        glu(2)
                    for c in channels:
                        tap = par[:, W_DW + c * WIDTH + k:W_DW + c * WIDTH + k + 1]
                        bias = par[:, B_DW + c:B_DW + c + 1]
                        if k > 0:
                            dve.wait_ge(dve_conv, last[c % 2])
                        if c == SHARED and k == WIDTH - 1:
                            dve.wait_ge(diag_used, len(pe_taps))
                            ins = V.tensor_tensor(z[:, c, :], z[:, c, :], ps[:, 3, :], ALU.add)
                        elif c == SHARED and k >= WIDTH - SHARED_TAPS:
                            continue
                        elif k == 0:
                            ins = V.tensor_scalar(z[:, c, :], uT[:, c, 0:S], tap, bias, ALU.mult, ALU.add)
                        else:
                            ins = V.scalar_tensor_tensor(out=z[:, c, :], in0=uT[:, c, k:k + S], scalar=tap,
                                                         in1=z[:, c, :], op0=ALU.mult, op1=ALU.add)
                        if k == WIDTH - 1:
                            ins.then_inc(z_ready, 1)
                        else:
                            ins.then_inc(dve_conv, 1)
                            taps += 1
                            last[c % 2] = taps
                if pair == 1:
                    glu(3)
            dve.wait_ge(mean_mm, 1)
            for c in range(KT):
                V.scalar_tensor_tensor(out=z[:, c, :], in0=ps[:, 2, :], scalar=-1.0 / D, in1=z[:, c, :],
                                       op0=ALU.mult, op1=ALU.add).then_inc(centred, 1)
            dve.wait_ge(lnroot_ready, 1)
            link.done(V.reciprocal(ln_scale, ln_root))

            def scale_z(k):
                V.tensor_tensor(z[:, k, :], z[:, k, :], ln_scale, ALU.mult).then_inc(zn_ready, 1)

            scale_z(0)
            scale_z(1)
            for k in range(KT):
                dve.wait_ge(hThi_ready, 2 * KT + k + 1)
                V.tensor_tensor(hT_lo[:, k, :], z[:, k, :], hT_hi[:, k, :].bitcast(F32), ALU.subtract) \
                    .then_inc(hTlo_ready, 1)
                if k + 2 < KT:
                    scale_z(k + 2)
            for n in range(2):
                for i in range(NT):
                    dve.wait_ge(pw2_mm, 4 * n + i + 1)
                    V.tensor_tensor(x[:, i, n * 512:(n + 1) * 512], x[:, i, n * 512:(n + 1) * 512],
                                    ps[:, 4 * n + i, :], ALU.add).then_inc(x2_added, 1)
            turned_x(3)
            expert_norm(1, 3)
            route(1, G_FFN + KT)
            expert_blocks(1, G_FFN + KT)
            dve.wait_ge(gfin_loaded, 16)
            combine(1, 4)


_NAMES = ("x_in", "pos_in", "const_in", "decay_in", "par_in", "w_in", "w_out", "w_pw1", "w_pw2", "b_pw2",
          "w_router", "b_router", "w_gate", "w_up", "w_down", "g_final")


def shape_constants():
    c = np.zeros((P, NCONST), np.float32)
    p = np.arange(P)
    c[:, C_ID:C_ID + P] = np.eye(P)
    c[:, C_TRI:C_TRI + P] = p[:, None] < p[None, :]
    c[:, C_ONE:C_ONE + P] = 1.0
    c[:, C_IOTA:C_IOTA + NBLK] = np.arange(NBLK)
    c[:, C_MOD:C_MOD + P] = p % BLK
    c[:, C_INV] = np.float32(10000.0) ** (-np.arange(P, dtype=np.float32) / np.float32(P))
    c[:, C_QOFF] = p // BLK - 4
    c[:, C_REV4:C_REV4 + NG] = NG - np.arange(NG)
    c[:, C_REV32:C_REV32 + NE] = NE - np.arange(NE)
    for j in range(8):
        tok = (j % NT) * P + p
        c[:, C_A + j] = 2 * tok + j // NT + 1
    gap = np.arange(S)[None, :] - p[:, None]
    decay = np.zeros((HEADS, P, S), np.float64)
    for h in range(HEADS):
        decay[h] = np.where(gap >= 0, (1.0 - 2.0 ** (-5.0 - h)) ** np.maximum(gap, 0), 0.0) * DK ** -0.5
    return c, decay.astype(np.float32)


def kernel(**inputs):
    import concourse.bacc as bacc
    from concourse.bass_utils import run_bass_kernel_spmd

    a = {k: np.asarray(v) for k, v in inputs.items()}
    const, decay = shape_constants()

    def columns(w):
        return w.reshape(-1, P).T

    taps = a["conv_w_dw"][0].reshape(WIDTH, KT, P).transpose(2, 1, 0).reshape(P, KT * WIDTH)
    par = np.concatenate([columns(a["norm_mix_g"]), columns(a["norm_ffn_g"]), columns(a["ret_head_g"]),
                          columns(a["conv_b_pw1"]), columns(a["conv_b_dw"]), columns(a["conv_ln_g"]),
                          columns(a["conv_ln_b"]), taps], axis=1)
    router = np.concatenate([a["moe_w_rg"], a["moe_w_re"]], axis=2).reshape(NL, KT, P, NG + NE)
    arrays = {
        "x_in": a["x"][0], "pos_in": a["positions"], "const_in": const, "decay_in": decay, "par_in": par,
        "w_in": a["ret_w_in"][0], "w_out": a["ret_w_out"][0], "w_pw1": a["conv_w_pw1"][0],
        "w_pw2": a["conv_w_pw2"][0], "b_pw2": a["conv_b_pw2"], "w_router": router.transpose(2, 0, 1, 3),
        "b_router": np.concatenate([a["moe_b_rg"], a["moe_b_re"]], axis=1).reshape(1, NL * (NG + NE)),
        "w_gate": a["moe_w_gate"], "w_up": a["moe_w_up"], "w_down": a["moe_w_down"],
        "g_final": a["final_norm_g"].reshape(1, D),
    }
    arrays = {k: np.ascontiguousarray(v) for k, v in arrays.items()}
    nc = bacc.Bacc("TRN2", target_bir_lowering=False, num_devices=1)
    aps = [nc.dram_tensor(n, arrays[n].shape, mybir.dt.from_np(arrays[n].dtype), kind="ExternalInput").ap()
           for n in _NAMES]
    out = nc.dram_tensor("out", (S, D), F32, kind="ExternalOutput").ap()
    program(nc, *aps, out)
    r = run_bass_kernel_spmd(nc, [arrays], core_ids=[0])
    return np.asarray(r.results[0]["out"]).reshape(1, S, D)
```
